# Optimizing a Trainium2 kernel written in Bass

```python
import math
import jax, jax.numpy as jnp
from jax import lax
import numpy as np
import jax
import jax.numpy as jnp

D_MODEL = 2048
BATCH = 1
SEQ = 256
DEPTH = 2

N_MIXERS = 4
WIDTH = D_MODEL
EPS = 1e-6
CONV_WIDTH = 31
HG_HEAD_DIM = 128
HG_HEADS = WIDTH // HG_HEAD_DIM
HG_CHUNK = 64
DA_HEAD_DIM = 128
DA_HEADS = WIDTH // (2 * DA_HEAD_DIM)
DA_V_DIM = 2 * DA_HEAD_DIM
ROPE_THETA = 500000.0
ROPE_DIM = DA_HEAD_DIM // 4
Q_BLOCK = 128
FN_GROUPS = 8
FN_GROUP_DIM = WIDTH // FN_GROUPS
N_CONV = len(range(0, DEPTH, N_MIXERS))
N_HGRN = len(range(1, DEPTH, N_MIXERS))
N_DIFF = len(range(2, DEPTH, N_MIXERS))
N_FNET = len(range(3, DEPTH, N_MIXERS))


def rms_norm(x, g):
    xf = x.astype(jnp.float32)
    y = xf * lax.rsqrt(jnp.mean(xf * xf, axis=-1, keepdims=True) + EPS)
    return (y * g.astype(jnp.float32)).astype(x.dtype)

def layer_norm(x, g, b):
    xf = x.astype(jnp.float32)
    mu = jnp.mean(xf, axis=-1, keepdims=True)
    var = jnp.mean(jnp.square(xf - mu), axis=-1, keepdims=True)
    y = (xf - mu) * lax.rsqrt(var + EPS)
    return (y * g.astype(jnp.float32) + b.astype(jnp.float32)).astype(x.dtype)

def conformer_conv(h, w_in, dw, dw_b, ln_g, ln_b, w_out):
    u = h @ w_in
    a, b, z = jnp.split(u, 3, axis=-1)
    v = a * jax.nn.sigmoid(b)
    pad = CONV_WIDTH // 2
    v = lax.conv_general_dilated(
        v, dw[:, None, :].astype(v.dtype), window_strides=(1,), padding=[(pad, pad)],
        dimension_numbers=("NWC", "WIO", "NWC"), feature_group_count=WIDTH) + dw_b
    v = jax.nn.silu(layer_norm(v, ln_g, ln_b))
    return (v * jax.nn.silu(z)) @ w_out

def hgrn_lower_bounds(table):
    lb = jnp.cumsum(jax.nn.softmax(table.astype(jnp.float32), axis=0), axis=0)
    return lb - lb[0:1]

def hgrn_direction(q, k, v, log_f):
    B, H, S, _ = q.shape
    nc = S // HG_CHUNK

    def chunks(t):
        return jnp.moveaxis(t.reshape(B, H, nc, HG_CHUNK, t.shape[-1]), 2, 0)

    lower_tri = jnp.tril(jnp.ones((HG_CHUNK, HG_CHUNK), dtype=bool))[:, :, None]

    def step(state, inp):
        qb, kb, vb, fb = inp
        b = jnp.cumsum(fb, axis=2)
        o_inter = jnp.einsum("bhtk,bhkv->bhtv", qb * jnp.exp(b), state)
        diff = b[:, :, :, None, :] - b[:, :, None, :, :]
        decay = jnp.exp(jnp.where(lower_tri, diff, -jnp.inf))
        scores = jnp.einsum("bhtk,bhsk,bhtsk->bhts", qb, kb, decay)
        o_intra = jnp.einsum("bhts,bhsv->bhtv", scores, vb)
        b_last = b[:, :, -1:, :]
        new_state = state * jnp.exp(b_last)[:, :, 0, :, None] + jnp.einsum(
            "bhsk,bhsv->bhkv", kb * jnp.exp(b_last - b), vb)
        return new_state, o_inter + o_intra

    state0 = jnp.zeros((B, H, q.shape[-1], v.shape[-1]), jnp.float32)
    _, out = lax.scan(step, state0, (chunks(q), chunks(k), chunks(v), chunks(log_f)))
    return jnp.moveaxis(out, 0, 2).reshape(B, H, S, v.shape[-1])

def hgrn2_mixer(h, w_in, lb_fwd, lb_bwd, o_norm, w_out):
    B, S, _ = h.shape
    u = h @ w_in
    q, a_f, a_b, i, z = jnp.split(u, 5, axis=-1)

    def heads(t):
        return t.astype(jnp.float32).reshape(B, S, HG_HEADS, HG_HEAD_DIM).transpose(0, 2, 1, 3)

    def forget(a, lb):
        a = a.astype(jnp.float32)
        log_f = jnp.logaddexp(jnp.log(lb), jnp.log1p(-lb) + jax.nn.log_sigmoid(a))
        key = (1.0 - lb) * jax.nn.sigmoid(-a)
        return heads(log_f), heads(key)

    qh, vh = heads(q), heads(i)
    lf_f, k_f = forget(a_f, lb_fwd)
    lf_b, k_b = forget(a_b, lb_bwd)
    o_fwd = hgrn_direction(qh, k_f, vh, lf_f)
    flip = lambda t: jnp.flip(t, axis=2)
    o_bwd = flip(hgrn_direction(flip(qh), flip(k_b), flip(vh), flip(lf_b)))
    o = rms_norm(o_fwd + o_bwd, o_norm)
    o = o.transpose(0, 2, 1, 3).reshape(B, S, WIDTH).astype(h.dtype)
    return (o * jax.nn.silu(z)) @ w_out

def rope_tables(positions):
    inv = 1.0 / (ROPE_THETA ** (jnp.arange(0, ROPE_DIM, 2, dtype=jnp.float32) / ROPE_DIM))
    ang = positions.astype(jnp.float32)[..., None] * inv
    return jnp.cos(ang), jnp.sin(ang)

def apply_partial_rope(x, cos, sin):
    xr, xp = x[..., :ROPE_DIM], x[..., ROPE_DIM:]
    x1, x2 = jnp.split(xr.astype(jnp.float32), 2, axis=-1)
    c = cos[:, :, None, None, :]
    s = sin[:, :, None, None, :]
    rot = jnp.concatenate([x1 * c - x2 * s, x2 * c + x1 * s], axis=-1)
    return jnp.concatenate([rot.astype(x.dtype), xp], axis=-1)

def diff_attention(h, cos, sin, w_in, q_norm, k_norm, lam_q1, lam_k1, lam_q2, lam_k2,
                   sub_norm, w_out, lam_init):
    B, S, _ = h.shape
    u = h @ w_in
    q, k, v, z = jnp.split(u, 4, axis=-1)
    q = rms_norm(q.reshape(B, S, DA_HEADS, 2, DA_HEAD_DIM), q_norm)
    k = rms_norm(k.reshape(B, S, DA_HEADS, 2, DA_HEAD_DIM), k_norm)
    q = apply_partial_rope(q, cos, sin).transpose(0, 2, 3, 1, 4)
    k = apply_partial_rope(k, cos, sin).transpose(0, 2, 3, 1, 4)
    v = v.reshape(B, S, DA_HEADS, DA_V_DIM).transpose(0, 2, 1, 3)
    f32 = jnp.float32
    lam = (jnp.exp(jnp.sum(lam_q1.astype(f32) * lam_k1.astype(f32)))
           - jnp.exp(jnp.sum(lam_q2.astype(f32) * lam_k2.astype(f32))) + lam_init)
    scale = 1.0 / math.sqrt(DA_HEAD_DIM)
    nq = S // Q_BLOCK
    qb_all = q.reshape(B, DA_HEADS, 2, nq, Q_BLOCK, DA_HEAD_DIM).transpose(3, 0, 1, 2, 4, 5)

    def block(qb):
        s = jnp.einsum("bhmqd,bhmkd->bhmqk", qb, k).astype(f32) * scale
        p = jax.nn.softmax(s, axis=-1)
        w = p[:, :, 0] - lam * p[:, :, 1]
        return jnp.einsum("bhqk,bhkv->bhqv", w.astype(v.dtype), v)

    o = lax.map(block, qb_all)
    o = o.transpose(1, 2, 0, 3, 4).reshape(B, DA_HEADS, S, DA_V_DIM)
    o = rms_norm(o, sub_norm) * (1.0 - lam_init)
    o = o.transpose(0, 2, 1, 3).reshape(B, S, WIDTH).astype(h.dtype)
    return (o * jax.nn.silu(z)) @ w_out

def fourier_mixer(h, w_in, group_w, w_out):
    B, S, _ = h.shape
    u = h @ w_in
    v, z = jnp.split(u, 2, axis=-1)
    vg = v.astype(jnp.float32).reshape(B, S, FN_GROUPS, FN_GROUP_DIM)
    f = jnp.fft.fftn(vg, axes=(1, 3), norm="ortho").real
    y = jnp.einsum("bsgc,gce->bsge", f.astype(h.dtype), group_w).reshape(B, S, WIDTH)
    return (y * jax.nn.silu(z)) @ w_out

def first_inputs(seed: int = 0) -> dict:
    key = jax.random.key(seed)
    ks = iter(jax.random.split(key, 40))
    E, D = WIDTH, D_MODEL
    nrm = lambda shape, s: jax.random.normal(next(ks), shape, jnp.float32) * s
    gain = lambda shape: 1.0 + nrm(shape, 0.02)
    return {
        "x": nrm((BATCH, SEQ, D), 1.0),
        "positions": jnp.broadcast_to(jnp.arange(SEQ, dtype=jnp.int32)[None, :], (BATCH, SEQ)),
        "conv_norm": gain((N_CONV, D)),
        "conv_w_in": nrm((N_CONV, D, 3 * E), D ** -0.5),
        "conv_dw": nrm((N_CONV, CONV_WIDTH, E), CONV_WIDTH ** -0.5),
        "conv_dw_b": nrm((N_CONV, E), 0.02),
        "conv_ln_g": gain((N_CONV, E)),
        "conv_ln_b": nrm((N_CONV, E), 0.02),
        "conv_w_out": nrm((N_CONV, E, D), E ** -0.5),
        "hgrn_norm": gain((N_HGRN, D)),
        "hgrn_w_in": nrm((N_HGRN, D, 5 * E), D ** -0.5),
        "hgrn_lb_fwd": nrm((DEPTH, E), 0.1),
        "hgrn_lb_bwd": nrm((DEPTH, E), 0.1),
        "hgrn_o_norm": gain((N_HGRN, HG_HEAD_DIM)),
        "hgrn_w_out": nrm((N_HGRN, E, D), E ** -0.5),
        "diff_norm": gain((N_DIFF, D)),
        "diff_w_in": nrm((N_DIFF, D, 4 * E), D ** -0.5),
        "diff_q_norm": gain((N_DIFF, DA_HEAD_DIM)),
        "diff_k_norm": gain((N_DIFF, DA_HEAD_DIM)),
        "diff_lam_q1": nrm((N_DIFF, DA_HEAD_DIM), 0.1),
        "diff_lam_k1": nrm((N_DIFF, DA_HEAD_DIM), 0.1),
        "diff_lam_q2": nrm((N_DIFF, DA_HEAD_DIM), 0.1),
        "diff_lam_k2": nrm((N_DIFF, DA_HEAD_DIM), 0.1),
        "diff_sub_norm": gain((N_DIFF, DA_V_DIM)),
        "diff_w_out": nrm((N_DIFF, E, D), E ** -0.5),
        "fnet_norm": gain((N_FNET, D)),
        "fnet_w_in": nrm((N_FNET, D, 2 * E), D ** -0.5),
        "fnet_group_w": nrm((N_FNET, FN_GROUPS, FN_GROUP_DIM, FN_GROUP_DIM), FN_GROUP_DIM ** -0.5),
        "fnet_w_out": nrm((N_FNET, E, D), E ** -0.5),
    }

def first_block(x, positions, conv_norm, conv_w_in, conv_dw, conv_dw_b, conv_ln_g, conv_ln_b, conv_w_out,
              hgrn_norm, hgrn_w_in, hgrn_lb_fwd, hgrn_lb_bwd, hgrn_o_norm, hgrn_w_out,
              diff_norm, diff_w_in, diff_q_norm, diff_k_norm, diff_lam_q1, diff_lam_k1, diff_lam_q2,
              diff_lam_k2, diff_sub_norm, diff_w_out,
              fnet_norm, fnet_w_in, fnet_group_w, fnet_w_out):
    cos, sin = rope_tables(positions)
    lb_fwd = hgrn_lower_bounds(hgrn_lb_fwd)
    lb_bwd = hgrn_lower_bounds(hgrn_lb_bwd)
    for layer in range(DEPTH):
        m, j = layer % N_MIXERS, layer // N_MIXERS
        if m == 0:
            h = rms_norm(x, conv_norm[j])
            y = conformer_conv(h, conv_w_in[j], conv_dw[j], conv_dw_b[j], conv_ln_g[j], conv_ln_b[j],
                               conv_w_out[j])
        elif m == 1:
            h = rms_norm(x, hgrn_norm[j])
            y = hgrn2_mixer(h, hgrn_w_in[j], lb_fwd[layer], lb_bwd[layer], hgrn_o_norm[j], hgrn_w_out[j])
        elif m == 2:
            h = rms_norm(x, diff_norm[j])
            lam_init = 0.8 - 0.6 * math.exp(-0.3 * layer)
            y = diff_attention(h, cos, sin, diff_w_in[j], diff_q_norm[j], diff_k_norm[j], diff_lam_q1[j],
                               diff_lam_k1[j], diff_lam_q2[j], diff_lam_k2[j], diff_sub_norm[j],
                               diff_w_out[j], lam_init)
        else:
            h = rms_norm(x, fnet_norm[j])
            y = fourier_mixer(h, fnet_w_in[j], fnet_group_w[j], fnet_w_out[j])
        x = x + y.astype(x.dtype)
    return x


DEPTH_2 = 1

NUM_MIXERS = 2

ATT_HEAD_DIM = 64
ATT_Q_HEADS = D_MODEL // ATT_HEAD_DIM
ATT_KV_HEADS = ATT_Q_HEADS // 8
ATT_GROUP = ATT_Q_HEADS // ATT_KV_HEADS
WINDOW = 128
ATT_BLOCK = WINDOW
ROPE_THETA_2 = 10000.0
QKV_WIDTH = (ATT_Q_HEADS + 2 * ATT_KV_HEADS) * ATT_HEAD_DIM

SSM_D_INNER = 2 * D_MODEL
SSM_HEAD_DIM = 64
SSM_HEADS = SSM_D_INNER // SSM_HEAD_DIM
SSM_GROUPS = 8
SSM_HEADS_PER_GROUP = SSM_HEADS // SSM_GROUPS
SSM_STATE = 128
SSM_CONV = 4
SSM_CHUNK = 256
SSM_CONV_DIM = SSM_D_INNER + 2 * SSM_GROUPS * SSM_STATE
SSM_IN_WIDTH = SSM_D_INNER + SSM_CONV_DIM + SSM_HEADS
SSM_NORM_GROUP = SSM_D_INNER // SSM_GROUPS

D_FF = -(-(8 * D_MODEL) // (3 * 256)) * 256

N_ATTN_LAYERS = (DEPTH_2 + NUM_MIXERS - 1) // NUM_MIXERS
N_SSM_LAYERS = DEPTH_2 // NUM_MIXERS


def rms_norm_2(x, gain):
    xf = x.astype(jnp.float32)
    y = xf * lax.rsqrt(jnp.mean(xf * xf, axis=-1, keepdims=True) + EPS)
    return (y * gain.astype(jnp.float32)).astype(x.dtype)

def rope_tables_2(positions):
    inv_freq = ROPE_THETA_2 ** (-jnp.arange(0, ATT_HEAD_DIM, 2, dtype=jnp.float32) / ATT_HEAD_DIM)
    ang = positions.astype(jnp.float32)[..., None] * inv_freq
    return jnp.cos(ang)[:, :, None, :], jnp.sin(ang)[:, :, None, :]

def apply_rope(t, cos, sin):
    tf = t.astype(jnp.float32)
    t1, t2 = jnp.split(tf, 2, axis=-1)
    return jnp.concatenate([t1 * cos - t2 * sin, t2 * cos + t1 * sin], axis=-1).astype(t.dtype)

def sliding_window_attention(h, positions, w_qkv, q_norm, k_norm, sinks, w_o):
    b, s, _ = h.shape
    qkv = h @ w_qkv
    q, k, v = jnp.split(qkv, [ATT_Q_HEADS * ATT_HEAD_DIM, (ATT_Q_HEADS + ATT_KV_HEADS) * ATT_HEAD_DIM], axis=-1)
    q = q.reshape(b, s, ATT_Q_HEADS, ATT_HEAD_DIM)
    k = k.reshape(b, s, ATT_KV_HEADS, ATT_HEAD_DIM)
    v = v.reshape(b, s, ATT_KV_HEADS, ATT_HEAD_DIM)
    q = rms_norm_2(q, q_norm)
    k = rms_norm_2(k, k_norm)
    cos, sin = rope_tables_2(positions)
    q = apply_rope(q, cos, sin)
    k = apply_rope(k, cos, sin)

    nb = s // ATT_BLOCK
    qb = q.reshape(b, nb, ATT_BLOCK, ATT_KV_HEADS, ATT_GROUP, ATT_HEAD_DIM)
    kb = k.reshape(b, nb, ATT_BLOCK, ATT_KV_HEADS, ATT_HEAD_DIM)
    vb = v.reshape(b, nb, ATT_BLOCK, ATT_KV_HEADS, ATT_HEAD_DIM)
    shift = ((0, 0), (1, 0), (0, 0), (0, 0), (0, 0))
    kw = jnp.concatenate([jnp.pad(kb, shift)[:, :-1], kb], axis=2)
    vw = jnp.concatenate([jnp.pad(vb, shift)[:, :-1], vb], axis=2)

    scale = ATT_HEAD_DIM ** -0.5
    scores = jnp.einsum('bnqhgd,bnkhd->bnhgqk', qb, kw).astype(jnp.float32) * scale
    qi = jnp.arange(ATT_BLOCK)[:, None]
    kj = jnp.arange(2 * ATT_BLOCK)[None, :]
    band = (kj > qi) & (kj <= qi + ATT_BLOCK)
    not_before_start = (jnp.arange(nb) > 0)[:, None, None] | (kj >= ATT_BLOCK)[None]
    valid = band[None] & not_before_start
    scores = jnp.where(valid[None, :, None, None], scores, -jnp.inf)

    sink = sinks.astype(jnp.float32).reshape(ATT_KV_HEADS, ATT_GROUP)[None, None, :, :, None, None]
    m = jnp.maximum(jnp.max(scores, axis=-1, keepdims=True), sink)
    p = jnp.exp(scores - m)
    probs = p / (jnp.sum(p, axis=-1, keepdims=True) + jnp.exp(sink - m))
    out = jnp.einsum('bnhgqk,bnkhd->bnqhgd', probs.astype(vw.dtype), vw)
    return out.reshape(b, s, ATT_Q_HEADS * ATT_HEAD_DIM) @ w_o

def causal_depthwise_conv(u, w, bias):
    out = lax.conv_general_dilated(u, w[:, None, :].astype(u.dtype), window_strides=(1,),
                                   padding=[(SSM_CONV - 1, 0)],
                                   dimension_numbers=('NWC', 'WIO', 'NWC'),
                                   feature_group_count=u.shape[-1])
    return out + bias.astype(u.dtype)

def mamba2_ssd(h, w_in, conv_w, conv_b, dt_bias, a_log, d_skip, norm_g, w_out):
    b, s, _ = h.shape
    G, R, P, N, L = SSM_GROUPS, SSM_HEADS_PER_GROUP, SSM_HEAD_DIM, SSM_STATE, SSM_CHUNK
    zxbcdt = h @ w_in
    z = zxbcdt[..., :SSM_D_INNER]
    xbc = zxbcdt[..., SSM_D_INNER:SSM_D_INNER + SSM_CONV_DIM]
    dt = zxbcdt[..., SSM_D_INNER + SSM_CONV_DIM:]
    xbc = jax.nn.silu(causal_depthwise_conv(xbc, conv_w, conv_b))
    xs, bm, cm = jnp.split(xbc, [SSM_D_INNER, SSM_D_INNER + G * N], axis=-1)

    xs = xs.astype(jnp.float32).reshape(b, s, G, R, P)
    bm = bm.astype(jnp.float32).reshape(b, s, G, N)
    cm = cm.astype(jnp.float32).reshape(b, s, G, N)
    dt = jax.nn.softplus(dt.astype(jnp.float32) + dt_bias.astype(jnp.float32)).reshape(b, s, G, R)
    a = -jnp.exp(a_log.astype(jnp.float32)).reshape(G, R)

    pad = (-s) % L
    nc = (s + pad) // L

    def to_chunks(t):
        t = jnp.pad(t, [(0, 0), (0, pad)] + [(0, 0)] * (t.ndim - 2))
        return jnp.moveaxis(t.reshape((b, nc, L) + t.shape[2:]), 1, 0)

    causal = jnp.tril(jnp.ones((L, L), dtype=bool))[None, :, :, None, None]

    def chunk_step(state, inp):
        xc, dtc, bc, cc = inp
        acum = jnp.cumsum(dtc * a, axis=1)
        seg = acum[:, :, None] - acum[:, None, :]
        decay = jnp.exp(jnp.where(causal, seg, -jnp.inf))
        xdt = xc * dtc[..., None]
        cb = jnp.einsum('blgn,bsgn->blsg', cc, bc)
        y_diag = jnp.einsum('blsgr,bsgrp->blgrp', cb[..., None] * decay, xdt)
        y_off = jnp.einsum('blgn,bgrpn->blgrp', cc, state) * jnp.exp(acum)[..., None]
        to_end = jnp.exp(acum[:, -1:] - acum)
        new_state = (state * jnp.exp(acum[:, -1])[..., None, None]
                     + jnp.einsum('bsgn,bsgr,bsgrp->bgrpn', bc, to_end, xdt))
        return new_state, y_diag + y_off

    init = jnp.zeros((b, G, R, P, N), jnp.float32)
    _, y = lax.scan(chunk_step, init, (to_chunks(xs), to_chunks(dt), to_chunks(bm), to_chunks(cm)))
    y = jnp.moveaxis(y, 0, 1).reshape(b, nc * L, G, R, P)[:, :s]
    y = y + d_skip.astype(jnp.float32).reshape(G, R)[:, :, None] * xs
    y = y.reshape(b, s, SSM_D_INNER) * jax.nn.silu(z.astype(jnp.float32))
    y = y.reshape(b, s, G, SSM_NORM_GROUP)
    y = y * lax.rsqrt(jnp.mean(y * y, axis=-1, keepdims=True) + EPS)
    y = y.reshape(b, s, SSM_D_INNER) * norm_g.astype(jnp.float32)
    return y.astype(h.dtype) @ w_out

def swiglu(h, w_gate, w_up, w_down):
    return (jax.nn.silu(h @ w_gate) * (h @ w_up)) @ w_down

def second_inputs(seed: int = 0) -> dict:
    key = jax.random.key(seed)
    ks = jax.random.split(key, 24)
    f32 = jnp.float32
    resid = (2 * DEPTH_2) ** -0.5

    def nrm(k, shape, fan_in, scale=1.0):
        return jax.random.normal(k, shape, f32) * (scale * fan_in ** -0.5)

    def gain(k, shape):
        return 1.0 + 0.02 * jax.random.normal(k, shape, f32)

    x = jax.random.normal(ks[0], (BATCH, SEQ, D_MODEL), f32)
    start = jax.random.randint(ks[1], (BATCH, 1), 0, 4096)
    positions = (start + jnp.arange(SEQ)[None, :]).astype(jnp.int32)

    dt0 = jnp.exp(jax.random.uniform(ks[14], (N_SSM_LAYERS, SSM_HEADS), f32)
                  * (math.log(0.1) - math.log(0.001)) + math.log(0.001))
    return {
        'x': x,
        'positions': positions,
        'mixer_norm': gain(ks[2], (DEPTH_2, D_MODEL)),
        'ffn_norm': gain(ks[3], (DEPTH_2, D_MODEL)),
        'attn_w_qkv': nrm(ks[4], (N_ATTN_LAYERS, D_MODEL, QKV_WIDTH), D_MODEL),
        'attn_q_norm': gain(ks[5], (N_ATTN_LAYERS, ATT_HEAD_DIM)),
        'attn_k_norm': gain(ks[6], (N_ATTN_LAYERS, ATT_HEAD_DIM)),
        'attn_sinks': 0.5 * jax.random.normal(ks[7], (N_ATTN_LAYERS, ATT_Q_HEADS), f32),
        'attn_w_o': nrm(ks[8], (N_ATTN_LAYERS, ATT_Q_HEADS * ATT_HEAD_DIM, D_MODEL), ATT_Q_HEADS * ATT_HEAD_DIM, resid),
        'ssm_w_in': nrm(ks[9], (N_SSM_LAYERS, D_MODEL, SSM_IN_WIDTH), D_MODEL),
        'ssm_conv_w': nrm(ks[10], (N_SSM_LAYERS, SSM_CONV, SSM_CONV_DIM), SSM_CONV),
        'ssm_conv_b': 0.02 * jax.random.normal(ks[11], (N_SSM_LAYERS, SSM_CONV_DIM), f32),
        'ssm_dt_bias': dt0 + jnp.log(-jnp.expm1(-dt0)),
        'ssm_a_log': jnp.log(jax.random.uniform(ks[12], (N_SSM_LAYERS, SSM_HEADS), f32, 1.0, 16.0)),
        'ssm_d': gain(ks[13], (N_SSM_LAYERS, SSM_HEADS)),
        'ssm_norm': gain(ks[15], (N_SSM_LAYERS, SSM_D_INNER)),
        'ssm_w_out': nrm(ks[16], (N_SSM_LAYERS, SSM_D_INNER, D_MODEL), SSM_D_INNER, resid),
        'ffn_w_gate': nrm(ks[17], (DEPTH_2, D_MODEL, D_FF), D_MODEL),
        'ffn_w_up': nrm(ks[18], (DEPTH_2, D_MODEL, D_FF), D_MODEL),
        'ffn_w_down': nrm(ks[19], (DEPTH_2, D_FF, D_MODEL), D_FF, resid),
    }

def second_block(x, positions, mixer_norm, ffn_norm, attn_w_qkv, attn_q_norm, attn_k_norm, attn_sinks,
              attn_w_o, ssm_w_in, ssm_conv_w, ssm_conv_b, ssm_dt_bias, ssm_a_log, ssm_d, ssm_norm,
              ssm_w_out, ffn_w_gate, ffn_w_up, ffn_w_down):
    for i in range(DEPTH_2):
        h = rms_norm_2(x, mixer_norm[i])
        j = i // NUM_MIXERS
        if i % NUM_MIXERS == 0:
            x = x + sliding_window_attention(h, positions, attn_w_qkv[j], attn_q_norm[j], attn_k_norm[j],
                                             attn_sinks[j], attn_w_o[j])
        else:
            x = x + mamba2_ssd(h, ssm_w_in[j], ssm_conv_w[j], ssm_conv_b[j], ssm_dt_bias[j], ssm_a_log[j],
                               ssm_d[j], ssm_norm[j], ssm_w_out[j])
        x = x + swiglu(rms_norm_2(x, ffn_norm[i]), ffn_w_gate[i], ffn_w_up[i], ffn_w_down[i])
    return x


def setup_inputs(seed=0):
    out = dict(first_inputs(seed))
    for name, value in second_inputs(seed + 1).items():
        if name != "x":
            out[name + "_2"] = value
    return out


def reference(
    x, positions, conv_norm, conv_w_in, conv_dw, conv_dw_b, conv_ln_g, conv_ln_b, conv_w_out,
    hgrn_norm, hgrn_w_in, hgrn_lb_fwd, hgrn_lb_bwd, hgrn_o_norm, hgrn_w_out, diff_norm,
    diff_w_in, diff_q_norm, diff_k_norm, diff_lam_q1, diff_lam_k1, diff_lam_q2, diff_lam_k2,
    diff_sub_norm, diff_w_out, fnet_norm, fnet_w_in, fnet_group_w, fnet_w_out, positions_2,
    mixer_norm_2, ffn_norm_2, attn_w_qkv_2, attn_q_norm_2, attn_k_norm_2, attn_sinks_2,
    attn_w_o_2, ssm_w_in_2, ssm_conv_w_2, ssm_conv_b_2, ssm_dt_bias_2, ssm_a_log_2, ssm_d_2,
    ssm_norm_2, ssm_w_out_2, ffn_w_gate_2, ffn_w_up_2, ffn_w_down_2,
):
    x = first_block(
        x, positions, conv_norm, conv_w_in, conv_dw, conv_dw_b, conv_ln_g, conv_ln_b,
        conv_w_out, hgrn_norm, hgrn_w_in, hgrn_lb_fwd, hgrn_lb_bwd, hgrn_o_norm, hgrn_w_out,
        diff_norm, diff_w_in, diff_q_norm, diff_k_norm, diff_lam_q1, diff_lam_k1, diff_lam_q2,
        diff_lam_k2, diff_sub_norm, diff_w_out, fnet_norm, fnet_w_in, fnet_group_w, fnet_w_out,
    )
    return second_block(
        x, positions_2, mixer_norm_2, ffn_norm_2, attn_w_qkv_2, attn_q_norm_2, attn_k_norm_2,
        attn_sinks_2, attn_w_o_2, ssm_w_in_2, ssm_conv_w_2, ssm_conv_b_2, ssm_dt_bias_2,
        ssm_a_log_2, ssm_d_2, ssm_norm_2, ssm_w_out_2, ffn_w_gate_2, ffn_w_up_2, ffn_w_down_2,
    )


_drawn_inputs = setup_inputs


def setup_inputs(seed=0):
    import zlib

    import numpy as np

    out = dict(_drawn_inputs(seed))
    spreads = {}
    factors = {'conv_norm': 3.629,
     'conv_dw_b': 2.884,
     'conv_ln_g': 4.503,
     'conv_ln_b': 5.29,
     'hgrn_o_norm': 5.939,
     'mixer_norm_2': 8.0,
     'ffn_norm_2': 6.002,
     'attn_q_norm_2': 8.0,
     'attn_k_norm_2': 8.0,
     'attn_sinks_2': 41.104}
    for name, (base, spread) in spreads.items():
        noise = np.random.default_rng([zlib.crc32(name.encode()), seed]).standard_normal(out[name].shape)
        drawn = base * np.exp(spread * noise) if base else spread * noise
        out[name] = jnp.asarray(drawn.astype(out[name].dtype))
    for name, factor in factors.items():
        out[name] = (out[name] * factor).astype(out[name].dtype)
    return out
```

```python
from contextlib import ExitStack

import numpy as np

import concourse.bass as bass
from concourse import mybir

F32 = mybir.dt.float32
F32R = mybir.dt.float32r
I32 = mybir.dt.int32
ACT = mybir.ActivationFunctionType
ALU = mybir.AluOpType
AX = mybir.AxisListType

P = 128
D = 2048
S = 256
TB = S // P
KT = D // P
GC = 512
CK = 2
CPG = KT // CK
SLOTS = 4
EPS = 1e-6
TAPS = 31
PAD = TAPS // 2
VP = S + 2 * PAD + 2
HPG = GC // P
HD = 64
QH = D // HD
KVH = QH // 8
D_FF = 5632
FKT = D_FF // P
FJ = D_FF // GC
FCH = FKT // CK
LEVELS = [64, 32, 16, 8, 4, 2, 1]
TWO_PI = 2 * np.pi
LN_MIN = 2.0 ** -64

(R_DWB, R_LNG, R_LNB, R_NORM0, R_NORM1, R_NORM2, R_NORM3, R_F0, R_F1, R_B0, R_B1) = range(TAPS, TAPS + 11)
ROWS = TAPS + 11


class Phase:

    def __init__(self, groups, per_iter, chunk0, uses0):
        self.per_iter, self.chunk0, self.uses0 = per_iter, chunk0, uses0
        self.uses_per = [(per_iter + 1) // 2, per_iter // 2]
        n = groups // per_iter
        self.chunk1 = chunk0 + groups * CPG
        self.uses1 = [uses0[p] + n * self.uses_per[p] for p in range(2)]

    def group(self, j, k):
        return Group(self.chunk0 + (j * self.per_iter + k) * CPG, k % 2,
                     self.uses0[k % 2] + j * self.uses_per[k % 2] + k // 2)


class Group:

    def __init__(self, chunk, pair, use):
        self.chunk, self.pair, self.use = chunk, pair, use
        self.done = chunk + CPG


def phases():
    out, chunk, uses = {}, 0, [0, 0]
    for name, groups, per in (("conv_ab", 8, 2), ("conv_z", 4, 4), ("conv_out", 4, 4), ("hgrn", 16, 4),
                              ("hgrn_z", 4, 4), ("hgrn_out", 4, 4), ("kv_q", 5, 5), ("att_out", 4, 4),
                              ("gate_up", 2 * FJ, 2)):
        ph = Phase(groups, per, chunk, uses)
        out[name] = ph
        chunk, uses = ph.chunk1, ph.uses1
    out["down"] = (chunk, uses)
    return out


def build(nc, t, out):
    ph = phases()
    ctx = ExitStack()
    with ctx:
        def sb(stack, name, shape, dt=F32):
            return stack.enter_context(nc.sbuf_tensor(name, shape, dt))

        def sem(name):
            return ctx.enter_context(nc.semaphore(name))

        raw = sb(ctx, "raw", [P, SLOTS, CK, GC])
        w_hi = sb(ctx, "w_hi", [P, SLOTS, CK, GC], F32R)
        w_lo = sb(ctx, "w_lo", [P, SLOTS, CK, GC], F32R)
        x = sb(ctx, "x", [P, TB, D])
        h_hi = sb(ctx, "h_hi", [P, KT, S], F32R)
        h_lo = sb(ctx, "h_lo", [P, KT, S], F32R)
        xs = sb(ctx, "xs", [P, 2, TB, 256])
        ident = sb(ctx, "ident", [P, P])
        feat = sb(ctx, "feat", [P, KT, ROWS])
        eps = sb(ctx, "eps", [P, 1])
        stat = sb(ctx, "stat", [P, 4, 2])
        mix = ExitStack()
        y_hi = sb(mix, "y_hi", [P, KT, S], F32R)
        ones = sb(mix, "ones", [P, P])
        lmask = sb(mix, "lmask", [P, len(LEVELS), P], I32)
        wmask = sb(mix, "wmask", [P, 3 * P])
        inv_freq = sb(mix, "inv_freq", [P, HD // 2])
        onorm = sb(mix, "onorm", [P, P])
        qkn = sb(mix, "qkn", [P, 2, HD])
        sinks = sb(mix, "sinks", [P, QH])
        posi = sb(mix, "posi", [P, TB], I32)
        lbt = sb(mix, "lbt", [P, 2, 2, KT])
        conv_s = ExitStack()
        y_lo = sb(conv_s, "y_lo", [P, KT, S], F32R)
        vpad = sb(conv_s, "vpad", [P, KT, VP])
        cy = sb(conv_s, "cy", [P, KT, S])
        szt = sb(conv_s, "szt", [P, KT, S])
        atok = sb(conv_s, "atok", [P, TB, GC])
        sg = sb(conv_s, "sg", [P, TB, GC])
        rows = cy[0:ROWS, 0:8, :].rearrange("p a b -> p (a b)")
        szt_std = sb(conv_s, "ln_std", [P, S])[:, :]
        lnr = sb(conv_s, "ln_rstd", [P, S])[:, :]
        conv_s.close()
        hs = ExitStack()
        o_all = sb(hs, "o_all", [P, 4, TB, GC])
        qtok = sb(hs, "qtok", [P, TB, GC])
        aftok = sb(hs, "aftok", [P, TB, GC])
        abtok = sb(hs, "abtok", [P, TB, GC])
        vtok = sb(hs, "vtok", [P, TB, GC])
        sz = sb(hs, "sz", [P, TB, GC])
        qT = sb(hs, "qT", [P, HPG, S])
        kf = sb(hs, "kf", [P, HPG, S])
        kb = sb(hs, "kb", [P, HPG, S])
        Bc = sb(hs, "Bc", [P, HPG, S])
        Xc = sb(hs, "Xc", [P, HPG, S])
        E = sb(hs, "E", [P, 2, HPG, S])
        ST = sb(hs, "ST", [P, 2, HPG, 2, P])
        ssh = sb(hs, "ssh", [P, 3, 2 * HPG])
        hs.close()
        yl2 = ExitStack()
        hy_lo = sb(yl2, "hy_lo", [P, KT, S], F32R)
        kvtok = sb(yl2, "kvtok", [P, TB, GC])
        aq = sb(yl2, "aq", [P, TB, GC])
        asq = sb(yl2, "asq", [P, TB, GC])
        ar = sb(yl2, "ar", [P, TB, GC])
        kdup = sb(yl2, "kdup", [P, TB, KVH, 2, HD])
        kT = sb(yl2, "kT", [P, KVH, S])
        aqT = sb(yl2, "aqT", [P, 4, S])
        sm = sb(yl2, "sm", [P, 8, 3 * P])
        PT = sb(yl2, "PT", [P, 2, 3 * P])
        cs = sb(yl2, "cs", [P, 2, TB, HD // 2])
        ang = sb(yl2, "ang", [P, 3, TB, HD // 2])
        posf = sb(yl2, "posf", [P, TB])
        ast = sb(yl2, "ast", [P, 8, 16])
        yl2.close()
        mix.close()
        f_hi = sb(ctx, "f_hi", [P, FKT, S], F32R)
        f_lo = sb(ctx, "f_lo", [P, FKT, S], F32R)
        fg = xs[:, :, :, :].rearrange("p a b c -> p a (b c)")

        acc = ctx.enter_context(nc.psum_tensor("acc", [P, 2, TB, GC], F32))
        T = ctx.enter_context(nc.psum_tensor("T", [P, 4, 512], F32))
        T01 = T[:, 0:2, :]
        T23 = T[:, 2:4, :]

        raw_in = [sem(f"raw_in{s}") for s in range(SLOTS)]
        hi_ready, split_ready, chunk_used = sem("hi_ready"), sem("split_ready"), sem("chunk_used")
        pair_free = [sem("pair_free0"), sem("pair_free1")]
        small_in, table_in, x_in = sem("small_in"), sem("table_in"), sem("x_in")
        const_ready, feat_T, feat_ready = sem("const_ready"), sem("feat_T"), sem("feat_ready")
        lb_diff, lb_ready = sem("lb_diff"), sem("lb_ready")
        x_done = sem("x_done")
        n_std, n_rstd, n_xs, n_T, n_hi, n_lo = (sem(f"norm_{s}") for s in ("std", "rstd", "xs", "T", "hi", "lo"))
        c_a, c_sg, c_v, c_T, c_pad, c_tap, c_yTap = (sem(f"conv_{s}") for s in ("a", "sg", "v", "T", "pad", "tap", "all"))
        c_z, c_zT, c_zc, c_mean, c_d, c_sq, c_var, c_std, c_n, c_act, c_g, c_hi, c_lo = (
            sem(f"ln_{s}") for s in ("z", "zT", "zc", "mean", "d", "sq", "var", "std", "n", "act", "g", "hi", "lo"))
        g_raw, g_T, g_act, g_aff, g_scan, g_D, g_E, g_G, g_mm, g_S = (
            sem(f"hgrn_{s}") for s in ("raw", "T", "act", "aff", "scan", "D", "E", "G", "mm", "S"))
        g_av, g_o, g_ss, g_std, g_on, g_z, g_y, g_yT, g_hi, g_lo = (
            sem(f"hgrn_{s}") for s in ("av", "o", "ss", "std", "on", "z", "y", "yT", "yhi", "ylo"))
        a_cs, a_ang, a_ev, a_sq, a_ss, a_std, a_rp, a_T, a_cp = (
            sem(f"att_{s}") for s in ("cs", "ang", "ev", "sq", "ss", "std", "rope", "T", "cp"))
        a_s, a_sm, a_m, a_p, a_pt, a_ptc, a_o, a_y, a_yT, a_hi, a_lo = (
            sem(f"att_{s}") for s in ("s", "sm", "m", "p", "pt", "ptc", "o", "y", "yT", "yhi", "ylo"))
        f_g, f_y, f_T, f_h, f_l = (sem(f"ffn_{s}") for s in ("g", "y", "T", "hi", "lo"))
        out_ready, out_done = sem("out_ready"), sem("out_done")

        def rounded(ap):
            return ap.bitcast(F32)

        def flat(ap):
            return ap.rearrange("p a b -> p (a b)")

        def cols(j, n=GC):
            return bass.ds(j * n, n)

        def use_of(n):
            return n // SLOTS + 1

        def tick_values(g, c):
            if isinstance(g.chunk, int):
                n = g.chunk + c
                return n, 16 * (n // SLOTS + 1)
            return g.chunk + c, g.chunk * (16 // SLOTS) + 16 * (c // SLOTS + 1)

        block = ctx.enter_context(nc.Block())

        @block.sync
        def _(sp):
            sp.dma_start(x[:, :, :], t["x"].rearrange("a (b p) d -> p (a b) d", p=P)).then_inc(x_in, 16)

            def chunk(W, n, slot, kt0, col, skip=False):
                if not skip:
                    sp.wait_ge(split_ready, n - SLOTS + 1)
                sp.dma_start(raw[:, slot, :, :], W[kt0 * P:(kt0 + CK) * P, bass.ds(col, GC)]
                             .rearrange("(k p) n -> p k n", p=P)).then_inc(raw_in[slot], 16)

            def group(W, g, col):
                for c in range(CPG):
                    chunk(W, g.chunk + c, c % SLOTS, c * CK, col,
                          skip=isinstance(g.chunk, int) and g.chunk + c < SLOTS)

            W = t["conv_w_in"][0]
            def ab(j):
                for k in range(2):
                    group(W, ph["conv_ab"].group(j, k), k * D + j * GC)
            ab(0)
            with sp.Fori(1, 4) as j:
                ab(j)
            for k in range(4):
                group(W, ph["conv_z"].group(0, k), 2 * D + k * GC)
            for k in range(4):
                group(t["conv_w_out"][0], ph["conv_out"].group(0, k), k * GC)
            W = t["hgrn_w_in"][0]
            with sp.Fori(0, 4) as j:
                for k in range(4):
                    group(W, ph["hgrn"].group(j, k), k * D + j * GC)
            for k in range(4):
                group(W, ph["hgrn_z"].group(0, k), 4 * D + k * GC)
            for k in range(4):
                group(t["hgrn_w_out"][0], ph["hgrn_out"].group(0, k), k * GC)
            for k in range(5):
                group(t["attn_w_qkv_2"][0], ph["kv_q"].group(0, k), D if k == 0 else (k - 1) * GC)
            for k in range(4):
                group(t["attn_w_o_2"][0], ph["att_out"].group(0, k), k * GC)
            with sp.Fori(0, FJ) as j:
                for k, W in enumerate((t["ffn_w_gate_2"][0], t["ffn_w_up_2"][0])):
                    group(W, ph["gate_up"].group(j, k), j * GC)
            n0 = ph["down"][0]
            for k in range(4):
                for c in range(FCH):
                    n = n0 + k * FCH + c
                    chunk(t["ffn_w_down_2"][0], n, n % SLOTS, c * CK, k * GC)
            for k in range(4):
                sp.wait_ge(out_ready, k + 1)
                sp.dma_start(out.rearrange("a (b p) d -> p (a b) d", p=P)[:, :, k * GC:(k + 1) * GC],
                             x[:, :, k * GC:(k + 1) * GC]).then_inc(out_done, 16)
            sp.wait_ge(out_done, 64)

        @block.gpsimd
        def _(pool):
            nc.gpsimd.memset(eps[:, :], EPS).then_inc(const_ready, 1)
            nc.gpsimd.memset(ones[:, :], 1.0 / D).then_inc(const_ready, 1)
            nc.gpsimd.memset(vpad[:, :, :], 0.0).then_inc(const_ready, 1)

        @block.tensor
        def _(pe):
            def transposes(dst, src_of, n=4):
                for q in range(n):
                    for tb in range(TB):
                        last = nc.tensor.transpose(
                            dst[:, q // 2, (q % 2) * S + tb * P:(q % 2) * S + tb * P + P], src_of(q, tb), ident[:, :])
                return last

            def tok(src):
                return lambda q, tb: src[:, tb, q * P:(q + 1) * P]

            def mms(o, hi, lo, kt, tb, slot, kk, first, end):
                a = slice(tb * P, (tb + 1) * P)
                nc.tensor.matmul(o, hi[:, kt, a], w_hi[:, slot, kk, :], start=first, stop=False)
                nc.tensor.matmul(o, hi[:, kt, a], w_lo[:, slot, kk, :], start=False, stop=False)
                return nc.tensor.matmul(o, lo[:, kt, a], w_hi[:, slot, kk, :], start=False, stop=end)

            def group(g, hi, lo, after={}):
                for c in range(CPG):
                    pe.wait_ge(split_ready, g.chunk + c + 1)
                    if c == 0 and not (isinstance(g.use, int) and g.use == 0):
                        pe.wait_ge(pair_free[g.pair], 2 * g.use)
                    for kk in range(CK):
                        for tb in range(TB):
                            kt = c * CK + kk
                            last = mms(acc[:, g.pair, tb, :], hi, lo, kt, tb, c % SLOTS, kk, kt == 0, kt == KT - 1)
                    last.then_inc(chunk_used, 1)
                    for f in after.get(c, ()):
                        f()

            def norm(s):
                for b in range(8):
                    pe.wait_ge(n_xs, 8 * s + b + 1)
                    if b >= 2:
                        pe.wait_ge(n_lo, 8 * s + b - 1)
                    for kk in range(2):
                        for tb in range(TB):
                            last = nc.tensor.transpose(T[:, b % 2, kk * S + tb * P:kk * S + tb * P + P],
                                                       xs[:, b % 2, tb, kk * P:(kk + 1) * P], ident[:, :])
                    last.then_inc(n_T, 1)
                pe.wait_ge(n_hi, 8 * s + 8)
                pe.wait_ge(n_lo, 8 * s + 8)

            pe.wait_ge(small_in, 16 * 11)
            for kt in range(KT):
                last = nc.tensor.transpose(T[:, kt // 8, (kt % 8) * ROWS:(kt % 8 + 1) * ROWS],
                                           rows[:, kt * P:(kt + 1) * P], ident[0:ROWS, 0:ROWS])
            last.then_inc(feat_T, 1)
            pe.wait_ge(feat_ready, 2)

            norm(0)

            def v_turn(j):
                pe.wait_ge(c_v, j + 1)
                if not (isinstance(j, int) and j == 0):
                    pe.wait_ge(c_pad, 2 * j)
                transposes(T01, tok(atok)).then_inc(c_T, 1)

            def ab(j):
                prev = {} if isinstance(j, int) and j == 0 else {4: [lambda: v_turn(j - 1)]}
                group(ph["conv_ab"].group(j, 0), h_hi, h_lo, prev)
                group(ph["conv_ab"].group(j, 1), h_hi, h_lo)
            ab(0)
            with pe.Fori(1, 4) as j:
                ab(j)

            def z_turn(k):
                pe.wait_ge(c_z, k + 1)
                if k == 0:
                    pe.wait_ge(c_pad, 8)
                else:
                    pe.wait_ge(c_zc, 2 * k)
                transposes(T01, tok(sg)).then_inc(c_zT, 1)
            for k in range(4):
                group(ph["conv_z"].group(0, k), h_hi, h_lo, {4: [(lambda: v_turn(3)) if k == 0 else (lambda k=k: z_turn(k - 1))]})
            z_turn(3)
            pe.wait_ge(c_yTap, 1)
            for kt in range(KT):
                last = nc.tensor.matmul(T[:, 2, 0:S], ones[:, :], cy[:, kt, :], start=kt == 0, stop=kt == KT - 1)
            last.then_inc(c_mean, 1)
            for q in range(4):
                pe.wait_ge(c_sq, q + 1)
                for i in range(4):
                    last = nc.tensor.matmul(T[:, 3, 0:S], ones[:, :], (atok, sg)[q % 2].rearrange("p a (b c) -> p (a b) c", c=S)[:, i, :],
                                            start=q == 0 and i == 0, stop=q == 3 and i == 3)
                last.then_inc(c_var, 1)
            pe.wait_ge(c_lo, 4)
            pe.wait_ge(c_hi, 4)
            for k in range(4):
                group(ph["conv_out"].group(0, k), y_hi, y_lo)

            norm(1)

            def turn(j, i, src, need):
                pe.wait_ge(g_raw, 4 * j + need)
                if i:
                    pe.wait_ge(g_act, 5 * j + (2, 4)[i - 1] - 1)
                elif not (isinstance(j, int) and j == 0):
                    pe.wait_ge(g_o, 2 * j)
                transposes(T01, tok(src)).then_inc(g_T, 1)

            def level(j, l):
                if l == 1:
                    pe.wait_ge(g_G, 9 * j + 2)
                else:
                    pe.wait_ge(g_G, 9 * j + l + 1)
                if l == 0:
                    pass
                else:
                    pe.wait_ge(g_S, 9 * j + l)
                for h in range(HPG):
                    for b in range(2):
                        o = T[:, h // 2, (h % 2) * S + b * P:(h % 2) * S + b * P + P]
                        sl = slice(b * P, (b + 1) * P)
                        tl = slice((1 - b) * P, (2 - b) * P) if l == 0 else sl
                        q = qT[:, h, tl] if l == 1 else E[:, 1, h, tl]
                        last = nc.tensor.matmul(o, E[:, 0, h, sl], q, start=True, stop=True)
                last.then_inc(g_mm, 1)

            def av(j):
                pe.wait_ge(g_S, 9 * j + 9)
                for h in range(HPG):
                    v = lambda s: vtok[:, s, h * P:(h + 1) * P]
                    for tb in range(TB):
                        o = T[:, tb, h * P:(h + 1) * P]
                        nc.tensor.matmul(o, ST[:, 1, h, tb, :], v(tb), start=True, stop=False)
                        last = nc.tensor.matmul(o, ST[:, 0, h, 1 - tb, :], v(1 - tb), start=False, stop=True)
                last.then_inc(g_av, 1)

            def process(j):
                at = {0: [lambda: turn(j, 0, qtok, 1)], 2: [lambda: turn(j, 1, aftok, 2)],
                      4: [lambda: turn(j, 2, abtok, 3)], 28: [lambda: av(j)]}
                for l in range(9):
                    at.setdefault(10 + 2 * l, []).insert(0, lambda l=l: level(j, l))
                return at

            def part(at, k):
                return {c: at[8 * k + c] for c in range(8) if 8 * k + c in at}

            def qaai(j):
                at = {} if isinstance(j, int) and j == 0 else process(j - 1)
                for k in range(4):
                    group(ph["hgrn"].group(j, k), h_hi, h_lo, part(at, k))
            qaai(0)
            with pe.Fori(1, 4) as j:
                qaai(j)

            def gated_turn(k):
                pe.wait_ge(g_y, k + 1)
                if k:
                    pe.wait_ge(g_lo, 2 * k)
                transposes(T23, tok(sz)).then_inc(g_yT, 1)
            at = process(3)
            for k in range(3):
                at.setdefault(8 * k + 12, []).append(lambda k=k: gated_turn(k))
            for k in range(4):
                group(ph["hgrn_z"].group(0, k), h_hi, h_lo, part(at, k))
            gated_turn(3)
            pe.wait_ge(g_lo, 8)
            for k in range(4):
                group(ph["hgrn_out"].group(0, k), y_hi, hy_lo)

            norm(2)

            def k_turn():
                pe.wait_ge(a_rp, 1)
                for h in range(KVH):
                    for tb in range(TB):
                        last = nc.tensor.transpose(T[:, h // 2, (h % 2) * S + tb * P:(h % 2) * S + tb * P + P],
                                                   kdup[:, tb, h, :, :].rearrange("p a b -> p (a b)"), ident[:, :])
                last.then_inc(a_T, 1)

            def q_turn(g):
                pe.wait_ge(a_rp, g + 2)
                if g == 0:
                    pe.wait_ge(a_cp, 2)
                else:
                    pe.wait_ge(a_lo, 2 * g)
                transposes(T01, tok(ar)).then_inc(a_T, 1)

            def scores(g, half):
                pe.wait_ge(a_cp, 2 * (g + 2))
                if half:
                    pe.wait_ge(a_sm, 8 * g + 4)
                elif g:
                    pe.wait_ge(a_y, g)
                for h in range(4 * half, 4 * half + 4):
                    r = slice(HD * (h % 2), HD * (h % 2) + HD)
                    nc.tensor.matmul(T[:, h % 4, 0:P], aqT[r, h // 2, 0:P], kT[r, g, 0:P], start=True, stop=True)
                    nc.tensor.matmul(T[:, h % 4, P:3 * P], aqT[r, h // 2, P:S], kT[r, g, :], start=True,
                                     stop=True).then_inc(a_s, 1)

            def pv(g, half):
                def turn_p(h):
                    pe.wait_ge(a_p, 8 * g + h + 1)
                    if 8 * g + h >= 2:
                        pe.wait_ge(a_ptc, 8 * g + h - 1)
                    if h < 2:
                        pe.wait_ge(a_sm, 8 * g + 8)
                    for i in range(3):
                        last = nc.tensor.transpose(T[:, h % 2, i * P:(i + 1) * P], sm[:, h, i * P:(i + 1) * P], ident[:, :])
                    last.then_inc(a_pt, 1)

                def mix_v(h):
                    pe.wait_ge(a_ptc, 8 * g + h + 1)
                    v = lambda tb: kvtok[:, tb, S + g * HD:S + (g + 1) * HD]
                    o = lambda tb: T[:, 2 + tb, h * HD:(h + 1) * HD]
                    nc.tensor.matmul(o(0), PT[:, h % 2, 0:P], v(0), start=True, stop=True)
                    nc.tensor.matmul(o(1), PT[:, h % 2, P:2 * P], v(0), start=True, stop=False)
                    nc.tensor.matmul(o(1), PT[:, h % 2, 2 * P:3 * P], v(1), start=False, stop=True).then_inc(a_o, 1)
                for h in range(4 * half, 4 * half + 4):
                    turn_p(h)
                    if h > 4 * half:
                        mix_v(h - 1)
                mix_v(4 * half + 3)

            def y_turn(g):
                pe.wait_ge(a_y, g + 1)
                transposes(T01, tok(ar)).then_inc(a_yT, 1)

            at = {12: [k_turn]}
            for g in range(4):
                for dt, f in ((4, lambda g=g: q_turn(g)), (5, lambda g=g: scores(g, 0)), (6, lambda g=g: scores(g, 1)),
                              (8, lambda g=g: pv(g, 0)), (9, lambda g=g: pv(g, 1)), (10, lambda g=g: y_turn(g))):
                    at.setdefault(16 + 8 * g + dt, []).append(f)
            for k in range(5):
                group(ph["kv_q"].group(0, k), h_hi, h_lo, part(at, k))
            for tick in range(40, 56):
                for f in at.get(tick, ()):
                    f()
            pe.wait_ge(a_lo, 8)
            for k in range(4):
                group(ph["att_out"].group(0, k), y_hi, hy_lo)

            norm(3)

            def f_turn(j):
                pe.wait_ge(f_y, j + 1)
                if not (isinstance(j, int) and j == 0):
                    pe.wait_ge(f_l, 2 * j)
                transposes(T01, tok(fg)).then_inc(f_T, 1)

            def gu(j):
                first = isinstance(j, int) and j == 0
                group(ph["gate_up"].group(j, 0), h_hi, h_lo, {} if first else {4: [lambda: f_turn(j - 1)]})
                group(ph["gate_up"].group(j, 1), h_hi, h_lo)
            gu(0)
            with pe.Fori(1, FJ) as j:
                gu(j)
            f_turn(FJ - 1)
            pe.wait_ge(f_l, 2 * FJ)
            n0, uses = ph["down"]
            for k in range(4):
                for c in range(FCH):
                    n = n0 + k * FCH + c
                    pe.wait_ge(split_ready, n + 1)
                    if c == 0:
                        pe.wait_ge(pair_free[k % 2], 2 * (uses[k % 2] + k // 2))
                    for kk in range(CK):
                        for tb in range(TB):
                            kt = c * CK + kk
                            last = mms(acc[:, k % 2, tb, :], f_hi, f_lo, kt, tb, n % SLOTS, kk, kt == 0, kt == FKT - 1)
                    last.then_inc(chunk_used, 1)

        @block.scalar
        def _(act):
            A = nc.scalar.activation

            def bcast(v, n):
                return v.partition_broadcast(n)
            vec = lambda name: t[name]
            for dst, src in ((rows[0:TAPS, :], t["conv_dw"][0]), (rows[R_DWB:R_DWB + 1, :], t["conv_dw_b"]),
                             (rows[R_LNG:R_LNG + 1, :], t["conv_ln_g"]), (rows[R_LNB:R_LNB + 1, :], t["conv_ln_b"]),
                             (rows[R_NORM0:R_NORM0 + 1, :], t["conv_norm"]), (rows[R_NORM1:R_NORM1 + 1, :], t["hgrn_norm"]),
                             (rows[R_NORM2:R_NORM2 + 1, :], t["mixer_norm_2"]), (rows[R_NORM3:R_NORM3 + 1, :], t["ffn_norm_2"]),
                             (rows[R_F0:R_F0 + 2, :], t["hgrn_lb_fwd"]), (rows[R_B0:R_B0 + 2, :], t["hgrn_lb_bwd"]),
                             (ident[:, :], t["c_ident"])):
                act.dma_start(dst, src).then_inc(small_in, 16)
            for dst, src in ((lmask[:, :, :], t["c_lmask"]), (wmask[:, :], t["c_wmask"]),
                             (inv_freq[:, :], t["c_inv_freq"][0].partition_broadcast(P)),
                             (onorm[:, :], t["hgrn_o_norm"][0].partition_broadcast(P)),
                             (qkn[:, 0, :], t["attn_q_norm_2"][0].partition_broadcast(P)),
                             (qkn[:, 1, :], t["attn_k_norm_2"][0].partition_broadcast(P)),
                             (sinks[:, :], t["attn_sinks_2"][0].partition_broadcast(P)),
                             (posi[:, :], t["positions_2"].rearrange("a (b p) -> p (a b)", p=P))):
                act.dma_start(dst, src, allow_slow_non_contiguous=True).then_inc(table_in, 16)

            def split(g, c):
                n, loads = tick_values(g, c)
                act.wait_ge(raw_in[c % SLOTS], loads)
                if not (isinstance(n, int) and n < SLOTS):
                    act.wait_ge(chunk_used, n - SLOTS + 1)
                A(w_hi[:, c % SLOTS, :, :], raw[:, c % SLOTS, :, :], ACT.Copy).then_inc(hi_ready, 1)

            def group(g, after={}):
                for c in range(CPG):
                    split(g, c)
                    for f in after.get(c, ()):
                        f()

            def part(at, k):
                return {c: at[8 * k + c] for c in range(8) if 8 * k + c in at}

            def evacuate(g, dst, func=ACT.Copy, done=None):
                act.wait_ge(chunk_used, g.done)
                for tb in range(TB):
                    A(dst[:, tb, :], acc[:, g.pair, tb, :], func).then_inc(pair_free[g.pair], 1)
                if done is not None:
                    nc.scalar.drain().then_inc(done, 1)

            def norm(s, row, xdone):
                if xdone is None:
                    act.wait_ge(x_in, 16)
                    act.wait_ge(const_ready, 3)
                else:
                    act.wait_ge(x_done, xdone)
                for tb in range(TB):
                    A(T[:, :, :].rearrange("p a b -> p (a b)"), x[:, tb, :], ACT.Square, accum_out=stat[:, 0, tb:tb + 1])
                    nc.scalar.drain()
                A(stat[:, 1, :], stat[:, 0, :], ACT.Sqrt, scale=1.0 / D, bias=eps[:, 0:1]).then_inc(n_std, 1)
                for b in range(8):
                    act.wait_ge(n_T, 8 * s + b + 1)
                    for kk in range(2):
                        kt = 2 * b + kk
                        last = A(h_hi[:, kt, :], T[:, b % 2, kk * S:(kk + 1) * S], ACT.Copy, scale=feat[:, kt, row:row + 1])
                    last.then_inc(n_hi, 1)

            act.wait_ge(feat_T, 1)
            for b in range(2):
                A(feat[:, 8 * b:8 * b + 8, :].rearrange("p a b -> p (a b)"), T[:, b, 0:8 * ROWS], ACT.Copy).then_inc(feat_ready, 1)
            act.wait_ge(lb_diff, 2)
            for d in range(2):
                A(lbt[:, d, 1, :], lbt[:, d, 0, :], ACT.Sigmoid, scale=-1.0)
                A(lbt[:, d, 0, :], lbt[:, d, 0, :], ACT.Sigmoid).then_inc(lb_ready, 1)

            norm(0, R_NORM0, None)

            def pad_copy(j):
                act.wait_ge(c_T, j + 1)
                for b in range(2):
                    A(vpad[:, bass.ds(4 * j + 2 * b, 2), PAD:PAD + S], T[:, b, :].rearrange("p (a b) -> p a b", a=2),
                      ACT.Copy).then_inc(c_pad, 1)

            def a_out(j):
                if not (isinstance(j, int) and j == 0):
                    act.wait_ge(c_T, j)
                evacuate(ph["conv_ab"].group(j, 0), atok, ACT.Copy, c_a)

            def b_out(j):
                evacuate(ph["conv_ab"].group(j, 1), sg, ACT.Sigmoid, c_sg)

            def ab(j):
                first = isinstance(j, int) and j == 0
                group(ph["conv_ab"].group(j, 0), {} if first else {2: [lambda: b_out(j - 1)], 7: [lambda: pad_copy(j - 1)]})
                group(ph["conv_ab"].group(j, 1), {2: [lambda: a_out(j)]})
            ab(0)
            with act.Fori(1, 4) as j:
                ab(j)

            def z_out(k):
                if k:
                    act.wait_ge(c_zT, k)
                evacuate(ph["conv_z"].group(0, k), sg, ACT.Silu, c_z)

            def z_copy(k):
                act.wait_ge(c_zT, k + 1)
                for b in range(2):
                    A(szt[:, 4 * k + 2 * b:4 * k + 2 * b + 2, :].rearrange("p a b -> p (a b)"), T[:, b, :],
                      ACT.Copy).then_inc(c_zc, 1)
            for k in range(4):
                group(ph["conv_z"].group(0, k), {2: [lambda: b_out(3)], 7: [lambda: pad_copy(3)]} if k == 0 else
                      {2: [lambda k=k: z_out(k - 1)], 7: [lambda k=k: z_copy(k - 1)]})
            z_out(3)
            z_copy(3)
            for q in range(4):
                act.wait_ge(c_d, q + 1)
                if q >= 2:
                    act.wait_ge(c_var, q - 1)
                A(flat((atok, sg)[q % 2]), flat(cy[:, 4 * q:4 * q + 4, :]), ACT.Square).then_inc(c_sq, 1)
            act.wait_ge(c_var, 4)
            A(szt_std, T[:, 3, 0:S], ACT.Sqrt, bias=eps[:, 0:1]).then_inc(c_std, 1)
            for q in range(4):
                act.wait_ge(c_n, q + 1)
                for kt in range(4 * q, 4 * q + 4):
                    last = A(cy[:, kt, :], cy[:, kt, :], ACT.Silu, scale=feat[:, kt, R_LNG:R_LNG + 1], bias=feat[:, kt, R_LNB:R_LNB + 1])
                last.then_inc(c_act, 1)
            for q in range(4):
                act.wait_ge(c_g, q + 1)
                A(y_hi[:, 4 * q:4 * q + 4, :], cy[:, 4 * q:4 * q + 4, :], ACT.Copy).then_inc(c_hi, 1)
            for k in range(4):
                group(ph["conv_out"].group(0, k))

            norm(1, R_NORM1, 8)

            def raw_out(j, k, dst):
                jj = isinstance(j, int) and j == 0
                if k < 3 and not jj:
                    act.wait_ge(g_T, 3 * (j - 1) + k + 1)
                if k == 3 and not jj:
                    act.wait_ge(g_av, j)
                evacuate(ph["hgrn"].group(j, k), dst, ACT.Copy, g_raw)

            def q_copy(j):
                act.wait_ge(g_T, 3 * j + 1)
                if not (isinstance(j, int) and j == 0):
                    act.wait_ge(g_mm, 9 * j)
                A(flat(qT[:, :, :]), flat(T01), ACT.Copy).then_inc(g_act, 1)

            def sig(j, d):
                act.wait_ge(g_T, 3 * j + 2 + d)
                k = (kf, kb)[d]
                s = Bc[:, :, :] if d == 0 else E[:, 0, :, :]
                A(flat(s), flat(T01), ACT.Sigmoid)
                A(flat(k[:, :, :]), flat(T01), ACT.Sigmoid, scale=-1.0).then_inc(g_act, 1)

            def ln(j, d):
                act.wait_ge(g_aff, 2 * j + d + 1)
                s = Bc[:, :, :] if d == 0 else E[:, 0, :, :]
                A(flat(s), flat(s), ACT.Ln).then_inc(g_act, 1)

            def exp(j, l):
                act.wait_ge(g_D, 8 * j + (l if l == 0 else l - 1) + 1)
                e = E[:, :, :, :].rearrange("p a b c -> p (a b c)")
                A(e, e, ACT.Exp).then_inc(g_E, 1)

            def o_out(j):
                act.wait_ge(g_av, j + 1)
                e = E[:, 0, :, :].rearrange("p a b -> p (a b)")
                A(e, flat(T01), ACT.Copy).then_inc(g_o, 1)
                A(E[:, 1, :, :].rearrange("p a b -> p (a b)"), flat(T01), ACT.Square).then_inc(g_o, 1)

            def o_std(j):
                act.wait_ge(g_ss, j + 1)
                A(ssh[:, 1, :], ssh[:, 0, :], ACT.Sqrt, scale=1.0 / P, bias=eps[:, 0:1]).then_inc(g_std, 1)

            def process(j):
                at = {1: [lambda: q_copy(j)], 3: [lambda: sig(j, 0)], 5: [lambda: ln(j, 0), lambda: sig(j, 1)],
                      7: [lambda: ln(j, 1)], 30: [lambda: o_out(j)], 31: [lambda: o_std(j)]}
                for l in range(9):
                    if l != 1:
                        at.setdefault(9 + 2 * l, []).append(lambda l=l: exp(j, l))
                return at

            def qaai(j):
                first = isinstance(j, int) and j == 0
                at = {} if first else process(j - 1)
                if not first:
                    at[0] = [lambda: raw_out(j - 1, 3, vtok)]
                for k, dst in enumerate((qtok, aftok, abtok)):
                    at.setdefault(8 * k + 10, []).insert(0, lambda k=k, dst=dst: raw_out(j, k, dst))
                for k in range(4):
                    group(ph["hgrn"].group(j, k), part(at, k))
            qaai(0)
            with act.Fori(1, 4) as j:
                qaai(j)

            def hz_out(k):
                if k:
                    act.wait_ge(g_yT, k)
                evacuate(ph["hgrn_z"].group(0, k), sz, ACT.Silu, g_z)

            def hz_hi(k):
                act.wait_ge(g_yT, k + 1)
                for b in range(2):
                    A(y_hi[:, 4 * k + 2 * b:4 * k + 2 * b + 2, :].rearrange("p a b -> p (a b)"), T[:, 2 + b, :],
                      ACT.Copy).then_inc(g_hi, 1)
            at = process(3)
            at[0] = [lambda: raw_out(3, 3, vtok)]
            for k in range(3):
                at.setdefault(8 * k + 10, []).append(lambda k=k: hz_out(k))
                at.setdefault(8 * k + 14, []).append(lambda k=k: hz_hi(k))
            for k in range(4):
                group(ph["hgrn_z"].group(0, k), part(at, k))
            hz_out(3)
            hz_hi(3)
            for k in range(4):
                group(ph["hgrn_out"].group(0, k))

            act.wait_ge(a_ang, 1)
            A(cs[:, 0, :, :].rearrange("p a b -> p (a b)"), ang[:, 0, :, :].rearrange("p a b -> p (a b)"), ACT.Sin)
            A(cs[:, 1, :, :].rearrange("p a b -> p (a b)"), ang[:, 1, :, :].rearrange("p a b -> p (a b)"), ACT.Sin).then_inc(a_cs, 1)
            norm(2, R_NORM2, 16)

            def q_out(g):
                if g >= 0:
                    act.wait_ge(a_rp, g + 1)
                evacuate(ph["kv_q"].group(0, g + 1), kvtok if g < 0 else aq, ACT.Copy, a_ev)
                w = KVH * HD if g < 0 else GC
                src = kvtok if g < 0 else aq
                A(asq[:, :, 0:w], src[:, :, 0:w], ACT.Square).then_inc(a_sq, 1)

            def q_std(g):
                act.wait_ge(a_ss, g + 2)
                w = 2 * KVH if g < 0 else 16
                A(ast[:, 1, 0:w], ast[:, 0, 0:w], ACT.Sqrt, scale=1.0 / HD, bias=eps[:, 0:1]).then_inc(a_std, 1)

            def qk_copy(g):
                act.wait_ge(a_T, g + 2)
                dst = kT if g < 0 else aqT
                for b in range(2):
                    A(dst[:, 2 * b:2 * b + 2, :].rearrange("p a b -> p (a b)"), T[:, b, :], ACT.Copy).then_inc(a_cp, 1)

            def exps(g):
                act.wait_ge(a_m, g + 1)
                for h in range(8):
                    A(sm[:, h, 0:P], sm[:, h, 0:P], ACT.Exp, bias=ast[:, 2, h:h + 1], accum_out=ast[:, 4, h:h + 1])
                    A(sm[:, h, P:3 * P], sm[:, h, P:3 * P], ACT.Exp, bias=ast[:, 2, 8 + h:9 + h],
                      accum_out=ast[:, 4, 8 + h:9 + h]).then_inc(a_p, 1)
                A(ast[:, 5, :], ast[:, 3, :], ACT.Exp).then_inc(a_p, 1) if False else A(ast[:, 5, :], ast[:, 3, :], ACT.Exp)
                nc.scalar.drain().then_inc(a_cs, 1)

            def p_copy(g, half):
                for h in range(4 * half, 4 * half + 4):
                    act.wait_ge(a_pt, 8 * g + h + 1)
                    if 8 * g + h >= 2:
                        act.wait_ge(a_o, 8 * g + h - 1)
                    A(PT[:, h % 2, :], T[:, h % 2, 0:3 * P], ACT.Copy).then_inc(a_ptc, 1)

            def y_out_hi(g):
                act.wait_ge(a_yT, g + 1)
                for b in range(2):
                    A(y_hi[:, 4 * g + 2 * b:4 * g + 2 * b + 2, :].rearrange("p a b -> p (a b)"), T[:, b, :],
                      ACT.Copy).then_inc(a_hi, 1)
            at = {}
            for g in range(-1, 4):
                for dt, f in ((2, lambda g=g: q_out(g)), (3, lambda g=g: q_std(g)), (5, lambda g=g: qk_copy(g))):
                    at.setdefault(16 + 8 * g + dt, []).append(f)
                if g >= 0:
                    for dt, f in ((7, lambda g=g: exps(g)), (8, lambda g=g: p_copy(g, 0)), (9, lambda g=g: p_copy(g, 1)),
                                  (11, lambda g=g: y_out_hi(g))):
                        at.setdefault(16 + 8 * g + dt, []).append(f)
            for k in range(5):
                group(ph["kv_q"].group(0, k), part(at, k))
            for tick in range(40, 56):
                for f in at.get(tick, ()):
                    f()
            for k in range(4):
                group(ph["att_out"].group(0, k))

            norm(3, R_NORM3, 24)

            def g_out(j):
                if not (isinstance(j, int) and j == 0):
                    act.wait_ge(f_T, j)
                evacuate(ph["gate_up"].group(j, 0), fg, ACT.Silu, f_g)

            def f_hi_out(j):
                act.wait_ge(f_T, j + 1)
                for b in range(2):
                    A(f_hi[:, bass.ds(4 * j + 2 * b, 2), :], T[:, b, :].rearrange("p (a b) -> p a b", a=2),
                      ACT.Copy).then_inc(f_h, 1)

            def gu(j):
                first = isinstance(j, int) and j == 0
                group(ph["gate_up"].group(j, 0), {} if first else {6: [lambda: f_hi_out(j - 1)]})
                group(ph["gate_up"].group(j, 1), {2: [lambda: g_out(j)]})
            gu(0)
            with act.Fori(1, FJ) as j:
                gu(j)
            f_hi_out(FJ - 1)
            n0 = ph["down"][0]
            for n in range(n0, n0 + 4 * FCH):
                act.wait_ge(raw_in[n % SLOTS], 16 * (n // SLOTS + 1))
                act.wait_ge(chunk_used, n - SLOTS + 1)
                A(w_hi[:, n % SLOTS, :, :], raw[:, n % SLOTS, :, :], ACT.Copy).then_inc(hi_ready, 1)

        @block.vector
        def _(dve):
            V = nc.vector
            TT = nc.vector.tensor_tensor

            def settle():
                return nc.vector.drain()

            def split(n, slot):
                dve.wait_ge(hi_ready, n + 1)
                TT(w_lo[:, slot, :, :], raw[:, slot, :, :], rounded(w_hi[:, slot, :, :]), ALU.subtract).then_inc(split_ready, 1)

            def group(g, after={}):
                for c in range(CPG):
                    split(g.chunk + c, c % SLOTS)
                    for f in after.get(c, ()):
                        f()

            def part(at, k):
                return {c: at[8 * k + c] for c in range(8) if 8 * k + c in at}

            def low(dst, src, hi, done):
                TT(dst, src, rounded(hi), ALU.subtract).then_inc(done, 1)

            def norm(s, row):
                dve.wait_ge(n_std, s + 1)
                V.reciprocal(stat[:, 2, :], stat[:, 1, :])
                settle()

                def scaled(b):
                    if b >= 2:
                        dve.wait_ge(n_T, 8 * s + b - 1)
                    for tb in range(TB):
                        last = V.tensor_scalar(xs[:, b % 2, tb, :], x[:, tb, b * 256:(b + 1) * 256], stat[:, 2, tb:tb + 1],
                                               None, ALU.mult)
                    last.then_inc(n_xs, 1)
                scaled(0)
                scaled(1)
                for b in range(8):
                    dve.wait_ge(n_hi, 8 * s + b + 1)
                    for kk in range(2):
                        kt = 2 * b + kk
                        last = V.scalar_tensor_tensor(out=h_lo[:, kt, :], in0=T[:, b % 2, kk * S:(kk + 1) * S],
                                                      scalar=feat[:, kt, row:row + 1], in1=rounded(h_hi[:, kt, :]),
                                                      op0=ALU.mult, op1=ALU.subtract)
                    last.then_inc(n_lo, 1)
                    if b + 2 < 8:
                        scaled(b + 2)

            def residual(g, k, done=None):
                dve.wait_ge(chunk_used, g.done)
                for tb in range(TB):
                    i = TT(x[:, tb, k * GC:(k + 1) * GC], acc[:, g.pair, tb, :], x[:, tb, k * GC:(k + 1) * GC], ALU.add)
                    i.then_inc(pair_free[g.pair], 1)
                settle().then_inc(done if done is not None else x_done, 1 if done is not None else 2)

            def out_projection(name):
                for k in range(4):
                    group(ph[name].group(0, k), {2: [lambda k=k: residual(ph[name].group(0, k - 1), k - 1)]} if k else {})
                residual(ph[name].group(0, 3), 3)

            dve.wait_ge(feat_ready, 2)
            for d, (r0, r1) in enumerate(((R_F0, R_F1), (R_B0, R_B1))):
                TT(lbt[:, d, 0, :], feat[:, :, r1], feat[:, :, r0], ALU.subtract).then_inc(lb_diff, 1)

            norm(0, R_NORM0)

            def v_out(j):
                dve.wait_ge(c_a, j + 1)
                dve.wait_ge(c_sg, j + 1)
                TT(atok[:, :, :], atok[:, :, :], sg[:, :, :], ALU.mult).then_inc(c_v, 1)

            def taps(j, lo, hi):
                for i in range(lo, hi):
                    tap, q = i // 4, i % 4
                    kt = bass.ds(4 * j + q, 1)
                    y = cy[:, kt, :].rearrange("p a b -> p (a b)")
                    v = vpad[:, kt, tap:tap + S].rearrange("p a b -> p (a b)")
                    w = feat[:, kt, tap:tap + 1].rearrange("p a b -> p (a b)")
                    if tap == 0:
                        if i == 0:
                            dve.wait_ge(c_pad, 2 * (j + 1))
                        bias = feat[:, kt, R_DWB:R_DWB + 1].rearrange("p a b -> p (a b)")
                        V.tensor_scalar(y, v, w, bias, ALU.mult, ALU.add).then_inc(c_tap, 1)
                    else:
                        dve.wait_ge(c_tap, j * (4 * TAPS) + i - 3)
                        V.scalar_tensor_tensor(out=y, in0=v, scalar=w, in1=y, op0=ALU.mult, op1=ALU.add).then_inc(c_tap, 1)

            def ab(j):
                first = isinstance(j, int) and j == 0
                group(ph["conv_ab"].group(j, 0), {} if first else {3: [lambda: v_out(j - 1)]})
                n = 4 * TAPS
                group(ph["conv_ab"].group(j, 1), {} if first else
                      {c: [lambda c=c: taps(j - 1, c * n // 8, (c + 1) * n // 8)] for c in range(8)})
            ab(0)
            with dve.Fori(1, 4) as j:
                ab(j)
            n = 4 * TAPS
            group(ph["conv_z"].group(0, 0), {3: [lambda: v_out(3)]})
            for k in range(1, 4):
                group(ph["conv_z"].group(0, k), {c: [lambda c=c, k=k: taps(3, (8 * (k - 1) + c) * n // 24, (8 * (k - 1) + c + 1) * n // 24)]
                                                  for c in range(8)})
            settle().then_inc(c_yTap, 1)
            dve.wait_ge(c_mean, 1)
            for q in range(4):
                p = cy[:, 4 * q:4 * q + 4, :]
                TT(p, p, T[:, 2, 0:S].unsqueeze(1).to_broadcast([P, 4, S]), ALU.subtract).then_inc(c_d, 1)
            dve.wait_ge(c_std, 1)
            V.reciprocal(lnr, szt_std)
            settle()
            for q in range(4):
                p = cy[:, 4 * q:4 * q + 4, :]
                TT(p, p, lnr.unsqueeze(1).to_broadcast([P, 4, S]), ALU.mult).then_inc(c_n, 1)
            dve.wait_ge(c_zc, 8)
            for q in range(4):
                dve.wait_ge(c_act, q + 1)
                p = cy[:, 4 * q:4 * q + 4, :]
                TT(p, p, szt[:, 4 * q:4 * q + 4, :], ALU.mult).then_inc(c_g, 1)
            for q in range(4):
                dve.wait_ge(c_hi, q + 1)
                low(y_lo[:, 4 * q:4 * q + 4, :], cy[:, 4 * q:4 * q + 4, :], y_hi[:, 4 * q:4 * q + 4, :], c_lo)
            out_projection("conv_out")

            norm(1, R_NORM1)
            dve.wait_ge(lb_ready, 2)
            dve.wait_ge(table_in, 16 * 8)

            def affine(j, d):
                dve.wait_ge(g_act, 5 * j + (2, 4)[d])
                k = (kf, kb)[d]
                s = Bc if d == 0 else E[:, 0, :, :]
                for h in range(HPG):
                    lb = lbt[:, d, 0, bass.ds(4 * j + h, 1)]
                    ob = lbt[:, d, 1, bass.ds(4 * j + h, 1)]
                    V.tensor_scalar(s[:, h, :], s[:, h, :], ob, lb, ALU.mult, ALU.add)
                    V.tensor_scalar(k[:, h, :], k[:, h, :], ob, None, ALU.mult)
                settle()
                s = s[:, :, :].rearrange("p a b -> p (a b)")
                V.tensor_scalar(s, s, LN_MIN, None, ALU.max).then_inc(g_aff, 1)

            def scans(j):
                dve.wait_ge(g_act, 5 * j + 5)
                for h in range(HPG):
                    V.tensor_tensor_scan(Bc[:, h, :], Bc[:, h, :], Bc[:, h, :], 0.0, ALU.add, ALU.bypass)
                    V.tensor_tensor_scan(Xc[:, h, 1:S], E[:, 0, h, 0:S - 1], E[:, 0, h, 0:S - 1], 0.0, ALU.add, ALU.bypass)
                V.memset(Xc[:, :, 0:1], 0.0)
                settle()

            def halves(a, c):
                v = a.rearrange("p h (b two c) -> p (h b) two c", two=2, c=c)
                return v[:, :, 0, :], v[:, :, 1, :]

            def bounds(c):
                n = HPG * S // (2 * c)
                f = halves(Bc[:, :, :], c)[0][:, :, c - 1:c]
                b = halves(Xc[:, :, :], c)[1][:, :, 0:1]
                return f.to_broadcast([P, n, c]), b.to_broadcast([P, n, c])

            def width(l):
                return P if l == 0 else LEVELS[l - 2]

            def diffs(j, l):
                if l:
                    dve.wait_ge(g_mm, 9 * j + l)
                if l == 1:
                    TT(E[:, 0, :, :], kf[:, :, :], kb[:, :, :], ALU.add).then_inc(g_G, 1)
                    return
                c = width(l)
                rf, rb = bounds(c)
                fl, fr = halves(Bc[:, :, :], c)
                bl, br = halves(Xc[:, :, :], c)
                gl, gr = halves(E[:, 0, :, :], c)
                ql, qr = halves(E[:, 1, :, :], c)
                TT(gl, rf, fl, ALU.subtract)
                TT(gr, br, rb, ALU.subtract)
                TT(ql, rb, bl, ALU.subtract)
                TT(qr, fr, rf, ALU.subtract).then_inc(g_D, 1)

            def weigh(j, l):
                dve.wait_ge(g_E, 8 * j + (l if l == 0 else l - 1) + 1)
                c = width(l)
                gl, gr = halves(E[:, 0, :, :], c)
                TT(gl, gl, halves(kf[:, :, :], c)[0], ALU.mult)
                TT(gr, gr, halves(kb[:, :, :], c)[1], ALU.mult)
                TT(E[:, 1, :, :], E[:, 1, :, :], qT[:, :, :], ALU.mult).then_inc(g_G, 1)

            def take(j, l):
                settle()
                dve.wait_ge(g_mm, 9 * j + l + 1)
                ps = flat(T01)
                if l < 2:
                    V.tensor_copy(ST[:, l, :, :, :].rearrange("p a b c -> p (a b c)"), ps).then_inc(g_S, 1)
                    return
                V.memset(stat[:, 3, :], 0.0)
                V.copy_predicated(ST[:, 1, :, :, :].rearrange("p a b c -> p (a b) c"),
                                  lmask[:, l - 2, :].unsqueeze(1).to_broadcast([P, 8, P]),
                                  ps.rearrange("p (a c) -> p a c", c=P)).then_inc(g_S, 1)

            def o_norm(j):
                dve.wait_ge(g_o, 2 * (j + 1))
                V.tensor_reduce(ssh[:, 0, :], E[:, 1, :, :].rearrange("p a (b c) -> p (a b) c", c=P), AX.X, ALU.add).then_inc(g_ss, 1)

            def o_scale(j):
                dve.wait_ge(g_std, j + 1)
                V.reciprocal(ssh[:, 2, :], ssh[:, 1, :])
                settle()
                e = E[:, 0, :, :].rearrange("p a (b c) -> p (a b) c", c=P)
                TT(e, e, ssh[:, 2, :].unsqueeze(2).to_broadcast([P, 8, P]), ALU.mult)
                settle()
                TT(o_all[:, bass.ds(j, 1), :, :].rearrange("p z a (b c) -> p (z a b) c", c=P), e,
                   onorm[:, :].unsqueeze(1).to_broadcast([P, 8, P]), ALU.mult).then_inc(g_on, 1)

            def process(j):
                at = {4: [lambda: affine(j, 0)], 6: [lambda: affine(j, 1)], 8: [lambda: scans(j)],
                      30: [lambda: o_norm(j)], 31: [lambda: o_scale(j)]}
                for l in range(9):
                    s = at.setdefault(9 + 2 * l, [])
                    if l:
                        s.append(lambda l=l: take(j, l - 1))
                    s.append(lambda l=l: diffs(j, l))
                    if l != 1:
                        at.setdefault(10 + 2 * l, []).append(lambda l=l: weigh(j, l))
                at.setdefault(28, []).append(lambda: take(j, 8))
                return at

            def qaai(j):
                at = {} if isinstance(j, int) and j == 0 else process(j - 1)
                for k in range(4):
                    group(ph["hgrn"].group(j, k), part(at, k))
            qaai(0)
            with dve.Fori(1, 4) as j:
                qaai(j)

            def gate(k):
                dve.wait_ge(g_on, k + 1)
                dve.wait_ge(g_z, k + 1)
                TT(sz[:, :, :], sz[:, :, :], o_all[:, k, :, :], ALU.mult).then_inc(g_y, 1)

            def z_lo(k):
                for b in range(2):
                    dve.wait_ge(g_hi, 2 * k + b + 1)
                    kk = slice(4 * k + 2 * b, 4 * k + 2 * b + 2)
                    low(hy_lo[:, kk, :].rearrange("p a b -> p (a b)"), T[:, 2 + b, :], y_hi[:, kk, :].rearrange("p a b -> p (a b)"), g_lo)
            at = process(3)
            for k in range(3):
                at.setdefault(8 * k + 11, []).append(lambda k=k: gate(k))
                at.setdefault(8 * k + 15, []).append(lambda k=k: z_lo(k))
            for k in range(4):
                group(ph["hgrn_z"].group(0, k), part(at, k))
            gate(3)
            z_lo(3)
            V.tensor_copy(posf[:, :], posi[:, :])
            settle()
            for tb in range(TB):
                V.tensor_scalar(ang[:, 2, tb, :], inv_freq[:, :], posf[:, tb:tb + 1], None, ALU.mult)
            settle()
            a2 = ang[:, 2, :, :].rearrange("p a b -> p (a b)")
            for i, shift in enumerate((np.pi / 2, 0.0)):
                a = ang[:, i, :, :].rearrange("p a b -> p (a b)")
                turns = cs[:, i, :, :].rearrange("p a b -> p (a b)")
                c1 = 6.28125
                c2 = float(np.float32(TWO_PI - c1) .view(np.uint32).__and__(np.uint32(0xFFFFF000)).view(np.float32))
                c3 = TWO_PI - c1 - c2
                magic = 1.5 * 2.0 ** 23
                V.tensor_scalar(turns, a2, 1 / TWO_PI, shift / TWO_PI, ALU.mult, ALU.add)
                settle()
                V.tensor_scalar(turns, turns, magic, None, ALU.add)
                settle()
                V.tensor_scalar(turns, turns, magic, None, ALU.subtract)
                settle()
                V.scalar_tensor_tensor(out=a, in0=turns, scalar=-c1, in1=a2, op0=ALU.mult, op1=ALU.add)
                settle()
                V.scalar_tensor_tensor(out=a, in0=turns, scalar=-c2, in1=a, op0=ALU.mult, op1=ALU.add)
                settle()
                V.scalar_tensor_tensor(out=a, in0=turns, scalar=-c3, in1=a, op0=ALU.mult, op1=ALU.add)
                settle()
                V.tensor_scalar(a, a, shift, None, ALU.add)
                settle()
                V.tensor_scalar(a, a, 3.1415925, -3.1415925, ALU.min, ALU.max)
            settle().then_inc(a_ang, 1)
            out_projection("hgrn_out")

            norm(2, R_NORM2)
            dve.wait_ge(a_cs, 1)

            def sums(g):
                dve.wait_ge(a_sq, g + 2)
                nh = KVH if g < 0 else 8
                V.tensor_reduce(ast[:, 0, 0:TB * nh].rearrange("p (a b) -> p a b", a=TB),
                                asq[:, :, 0:nh * HD].rearrange("p a (b c) -> p a b c", c=HD), AX.X, ALU.add).then_inc(a_ss, 1)

            def rope(g):
                dve.wait_ge(a_std, g + 2)
                nh = KVH if g < 0 else 8
                src = (kvtok if g < 0 else aq)[:, :, 0:nh * HD].rearrange("p a (b c) -> p a b c", c=HD)
                V.reciprocal(ast[:, 6, 0:TB * nh], ast[:, 1, 0:TB * nh])
                settle()
                for tb in range(TB):
                    s = src[:, tb, :, :]
                    TT(s, s, ast[:, 6, tb * nh:(tb + 1) * nh].unsqueeze(2).to_broadcast([P, nh, HD]), ALU.mult)
                settle()
                for tb in range(TB):
                    s = src[:, tb, :, :]
                    TT(s, s, qkn[:, 1 if g < 0 else 0, :].unsqueeze(1).to_broadcast([P, nh, HD]), ALU.mult)
                if g > 0:
                    dve.wait_ge(a_yT, g)
                settle()
                H2 = HD // 2
                for tb in range(TB):
                    c = cs[:, 0, tb, :].unsqueeze(1).to_broadcast([P, nh, H2])
                    s = cs[:, 1, tb, :].unsqueeze(1).to_broadcast([P, nh, H2])
                    dst = kdup[:, tb, :, 0, :] if g < 0 else ar[:, tb, :].rearrange("p (b c) -> p b c", c=HD)
                    tmp = asq[:, tb, 0:nh * HD].rearrange("p (b c) -> p b c", c=HD)
                    x1, x2 = src[:, tb, :, 0:H2], src[:, tb, :, H2:HD]
                    TT(dst[:, :, 0:H2], x1, c, ALU.mult)
                    TT(dst[:, :, H2:HD], x2, c, ALU.mult)
                    TT(tmp[:, :, 0:H2], x2, s, ALU.mult)
                    TT(tmp[:, :, H2:HD], x1, s, ALU.mult)
                    settle()
                    TT(dst[:, :, 0:H2], dst[:, :, 0:H2], tmp[:, :, 0:H2], ALU.subtract)
                    TT(dst[:, :, H2:HD], dst[:, :, H2:HD], tmp[:, :, H2:HD], ALU.add)
                    if g < 0:
                        settle()
                        V.tensor_copy(kdup[:, tb, :, 1, :], kdup[:, tb, :, 0, :])
                settle().then_inc(a_rp, 1)

            def masked(g, half):
                for h in range(4 * half, 4 * half + 4):
                    dve.wait_ge(a_s, 8 * g + h + 1)
                    if g and h == 0:
                        dve.wait_ge(a_pt, 8 * g)
                    V.scalar_tensor_tensor(out=sm[:, h, :], in0=T[:, h % 4, 0:3 * P], scalar=HD ** -0.5, in1=wmask[:, :],
                                           op0=ALU.mult, op1=ALU.add).then_inc(a_sm, 1)

            def maxima(g):
                settle()
                if g:
                    dve.wait_ge(a_cs, 1 + g)
                V.tensor_reduce(ast[:, 2, 0:8], sm[:, :, 0:P], AX.X, ALU.max)
                V.tensor_reduce(ast[:, 2, 8:16], sm[:, :, P:3 * P], AX.X, ALU.max)
                settle()
                sk = sinks[:, 8 * g:8 * g + 8].unsqueeze(1).to_broadcast([P, 2, 8])
                m = ast[:, 2, :].rearrange("p (a b) -> p a b", a=2)
                TT(m, m, sk, ALU.max)
                settle()
                TT(ast[:, 3, :].rearrange("p (a b) -> p a b", a=2), sk, m, ALU.subtract)
                settle()
                V.tensor_scalar(ast[:, 2, :], ast[:, 2, :], -1.0, None, ALU.mult).then_inc(a_m, 1)

            def finish(g):
                dve.wait_ge(a_o, 8 * g + 8)
                dve.wait_ge(a_cs, 2 + g)
                TT(ast[:, 7, :], ast[:, 4, :], ast[:, 5, :], ALU.add)
                settle()
                V.reciprocal(ast[:, 6, :], ast[:, 7, :])
                settle()
                TT(ar[:, :, :].rearrange("p a (b c) -> p (a b) c", c=HD), T[:, 2:4, :].rearrange("p a (b c) -> p (a b) c", c=HD),
                   ast[:, 6, :].unsqueeze(2).to_broadcast([P, 16, HD]), ALU.mult).then_inc(a_y, 1)

            def y_low(g):
                for b in range(2):
                    dve.wait_ge(a_hi, 2 * g + b + 1)
                    kk = slice(4 * g + 2 * b, 4 * g + 2 * b + 2)
                    low(hy_lo[:, kk, :].rearrange("p a b -> p (a b)"), T[:, b, :], y_hi[:, kk, :].rearrange("p a b -> p (a b)"), a_lo)
            at = {}
            for g in range(-1, 4):
                for dt, f in ((2, lambda g=g: sums(g)), (3, lambda g=g: rope(g))):
                    at.setdefault(16 + 8 * g + dt, []).append(f)
                if g >= 0:
                    for dt, f in ((6, lambda g=g: masked(g, 0)), (7, lambda g=g: masked(g, 1)), (7, lambda g=g: maxima(g)),
                                  (10, lambda g=g: finish(g)), (11, lambda g=g: y_low(g))):
                        at.setdefault(16 + 8 * g + dt, []).insert(0, f) if dt >= 10 else at.setdefault(16 + 8 * g + dt, []).append(f)
            for k in range(5):
                group(ph["kv_q"].group(0, k), part(at, k))
            for tick in range(40, 56):
                for f in at.get(tick, ()):
                    f()
            out_projection("att_out")

            norm(3, R_NORM3)

            def u_out(j):
                dve.wait_ge(f_g, j + 1)
                g = ph["gate_up"].group(j, 1)
                dve.wait_ge(chunk_used, g.done)
                for tb in range(TB):
                    TT(fg[:, tb, :], acc[:, g.pair, tb, :], fg[:, tb, :], ALU.mult).then_inc(pair_free[g.pair], 1)
                settle().then_inc(f_y, 1)

            def f_lo_out(j):
                for b in range(2):
                    dve.wait_ge(f_h, 2 * j + b + 1)
                    kk = bass.ds(4 * j + 2 * b, 2)
                    low(f_lo[:, kk, :], T[:, b, :].rearrange("p (a b) -> p a b", a=2), f_hi[:, kk, :], f_l)

            def gu(j):
                first = isinstance(j, int) and j == 0
                group(ph["gate_up"].group(j, 0), {} if first else {2: [lambda: u_out(j - 1)], 7: [lambda: f_lo_out(j - 1)]})
                group(ph["gate_up"].group(j, 1))
            gu(0)
            with dve.Fori(1, FJ) as j:
                gu(j)
            u_out(FJ - 1)
            f_lo_out(FJ - 1)
            n0 = ph["down"][0]
            for k in range(4):
                for c in range(FCH):
                    n = n0 + k * FCH + c
                    split(n, n % SLOTS)
                    if k and c == 2:
                        residual(Group(n0 + k * FCH - CPG, (k - 1) % 2, 0), k - 1, out_ready)
            residual(Group(n0 + 4 * FCH - CPG, 1, 0), 3, out_ready)


def constants():
    i = np.arange(P)
    levels = np.stack([((i[:, None] // (2 * c)) == (i[None] // (2 * c))) & ((i[:, None] // c) != (i[None] // c))
                       for c in LEVELS], 1).astype(np.int32)
    q, k = i[:, None], i[None]
    allowed = np.concatenate([k <= q, k > q, k <= q], 1)
    wmask = np.where(allowed, 0.0, -1e30).astype(np.float32)
    inv = (np.float32(10000.0) ** (-np.arange(0, HD, 2, dtype=np.float32) / np.float32(HD))).astype(np.float32)
    return {"c_ident": np.eye(P, dtype=np.float32), "c_lmask": levels, "c_wmask": wmask, "c_inv_freq": inv[None]}


_INS = ["x", "conv_norm", "conv_w_in", "conv_dw", "conv_dw_b", "conv_ln_g", "conv_ln_b", "conv_w_out", "hgrn_norm",
        "hgrn_w_in", "hgrn_lb_fwd", "hgrn_lb_bwd", "hgrn_o_norm", "hgrn_w_out", "positions_2", "mixer_norm_2",
        "ffn_norm_2", "attn_w_qkv_2", "attn_q_norm_2", "attn_k_norm_2", "attn_sinks_2", "attn_w_o_2", "ffn_w_gate_2",
        "ffn_w_up_2", "ffn_w_down_2"]


def kernel(**inputs):
    import concourse.bacc as _bacc
    from concourse.bass_utils import run_bass_kernel_spmd as _run

    nc = _bacc.Bacc("TRN2", target_bir_lowering=False, num_devices=1)
    arrays, handles = {}, {}
    given = {name: np.ascontiguousarray(inputs[name]) for name in _INS} | constants()
    for name, a in given.items():
        arrays[f"in_{name}_dram"] = a
        handles[name] = nc.dram_tensor(f"in_{name}_dram", a.shape, mybir.dt.from_np(a.dtype), kind="ExternalInput").ap()
    out = nc.dram_tensor("out_0_dram", (1, S, D), F32, kind="ExternalOutput").ap()
    build(nc, handles, out)
    r = _run(nc, [arrays], core_ids=[0])
    return r.results[0]["out_0_dram"]
```

```python
from contextlib import ExitStack

import numpy as np

import concourse.bass as bass
from concourse import mybir

F32 = mybir.dt.float32
F32R = mybir.dt.float32r
I32 = mybir.dt.int32
ACT = mybir.ActivationFunctionType
ALU = mybir.AluOpType
AX = mybir.AxisListType

P = 128
D = 2048
S = 256
TB = S // P
KT = D // P
GC = 512
CK = 2
CPG = KT // CK
SLOTS = 4
EPS = 1e-6
TAPS = 31
PE_TAPS = 6
DVE_TAPS = TAPS - PE_TAPS
STEPS = DVE_TAPS + 1
ADD_STEP = 14
PAD = TAPS // 2
VP = S + 2 * PAD + 2
HPG = GC // P
HD = 64
QH = D // HD
KVH = QH // 8
D_FF = 5632
FKT = D_FF // P
FJ = D_FF // GC
FCH = FKT // CK
LEVELS = [64, 32, 16, 8, 4, 2, 1]
TWO_PI = 2 * np.pi
LN_MIN = 2.0 ** -64

(R_DWB, R_LNG, R_LNB, R_NORM0, R_NORM1, R_NORM2, R_NORM3, R_F0, R_F1, R_B0, R_B1) = range(TAPS, TAPS + 11)
ROWS = TAPS + 11


class Phase:

    def __init__(self, iters, per_iter, chunk0, pair0, uses0, chunks=CPG, lead=0):
        self.chunk0, self.pair0, self.uses0 = chunk0, pair0, uses0
        assert iters == 1 or per_iter % 2 == 0
        self.uses_per = [sum(self.pair(k) == p for k in range(per_iter)) for p in range(2)]
        head = [(k, c) for cs in (range(chunks - 4), (chunks - 4, chunks - 3), (chunks - 2, chunks - 1))
                for k in range(lead) for c in cs]
        self.seq = head + [(k, c) for k in range(lead, per_iter) for c in range(chunks)]
        self.last = {k: i for i, (k, c) in enumerate(self.seq) if c == chunks - 1}
        self.chunks = chunks
        self.chunk1 = chunk0 + iters * len(self.seq)
        self.uses1 = [uses0[p] + iters * self.uses_per[p] for p in range(2)]

    def pair(self, k):
        return (self.pair0 + k) % 2

    def base(self, j):
        return self.chunk0 + j * len(self.seq)

    def done(self, j, k):
        return self.base(j) + self.last[k] + 1

    def use(self, j, k):
        return self.uses0[self.pair(k)] + j * self.uses_per[self.pair(k)] + k // 2

    def end(self, k):
        return self.last[k] + 1


def phases():
    out, chunk, pair, uses = {}, 0, 0, [0, 0]
    for name, iters, per, more in (
            ("conv_ab", 4, 2, {}), ("conv_z", 1, 4, {}), ("conv_out", 1, 4, {}), ("hgrn", 4, 4, {}),
            ("hgrn_z", 1, 4, {}), ("hgrn_out", 1, 4, {}), ("kv_q", 1, 5, {}), ("att_out", 1, 4, {"lead": 2}),
            ("gate_up", FJ, 2, {}), ("down", 1, 4, {"chunks": FCH})):
        out[name] = Phase(iters, per, chunk, pair, uses, **more)
        pair = out[name].pair(iters * per)
        chunk, uses = out[name].chunk1, out[name].uses1
    return out


def is_first(j):
    return isinstance(j, int) and j == 0


class Hooks(dict):

    def put(self, tick, step):
        self.setdefault(tick, []).append(step)
        return self

    def later(self, ticks):
        return Hooks({t - ticks: steps for t, steps in self.items() if t >= ticks})

    def with_(self, other):
        for t, steps in other.items():
            self.setdefault(t, []).extend(steps)
        return self


def build(nc, t, out):
    ph = phases()
    ctx = ExitStack()
    with ctx:
        def sb(stack, name, shape, dt=F32):
            return stack.enter_context(nc.sbuf_tensor(name, shape, dt))

        def sem(name):
            return ctx.enter_context(nc.semaphore(name))

        raw = sb(ctx, "raw", [P, SLOTS, CK, GC])
        w_hi = sb(ctx, "w_hi", [P, SLOTS, CK, GC], F32R)
        w_lo = sb(ctx, "w_lo", [P, SLOTS, CK, GC], F32R)
        x = sb(ctx, "x", [P, TB, D])
        h_hi = sb(ctx, "h_hi", [P, KT, S], F32R)
        h_lo = sb(ctx, "h_lo", [P, KT, S], F32R)
        fg = sb(ctx, "fg", [P, TB, GC])
        ident = sb(ctx, "ident", [P, P])
        feat = sb(ctx, "feat", [P, KT, ROWS])
        eps = sb(ctx, "eps", [P, 1])
        ssq = sb(ctx, "ssq", [P, TB, 4])
        rms = sb(ctx, "rms", [P, 2, TB])
        rs = sb(ctx, "rs", [P, 4, TB])
        none = sb(ctx, "none", [P, 2])
        mix = ExitStack()
        y_hi = sb(mix, "y_hi", [P, KT, S], F32R)
        ones = sb(mix, "ones", [P, P])
        lmask = sb(mix, "lmask", [P, len(LEVELS), P], I32)
        wmask = sb(mix, "wmask", [P, 3 * P])
        inv_freq = sb(mix, "inv_freq", [P, HD // 2])
        onorm = sb(mix, "onorm", [P, P])
        qkn = sb(mix, "qkn", [P, 2, HD])
        sinks = sb(mix, "sinks", [P, QH])
        posi = sb(mix, "posi", [P, TB], I32)
        lbt = sb(mix, "lbt", [P, 2, 2, KT])
        cs = sb(mix, "cs", [P, 2, TB, HD // 2])
        conv_s = ExitStack()
        taps_s = ExitStack()
        diag = sb(taps_s, "diag", [P, 2, PE_TAPS, P])
        taps_s.close()
        y_lo = sb(conv_s, "y_lo", [P, KT, S], F32R)
        vpad = sb(conv_s, "vpad", [P, KT, VP])
        cy = sb(conv_s, "cy", [P, KT, S])
        szt = sb(conv_s, "szt", [P, KT, S])
        atok = sb(conv_s, "atok", [P, TB, GC])
        sg = sb(conv_s, "sg", [P, TB, GC])
        rows = cy[0:ROWS, 0:8, :].rearrange("p a b -> p (a b)")
        ln_std = sb(conv_s, "ln_std", [P, S])
        ln_rstd = sb(conv_s, "ln_rstd", [P, S])
        conv_s.close()
        hs = ExitStack()
        o_all = sb(hs, "o_all", [P, 4, TB, GC])
        qtok = sb(hs, "qtok", [P, TB, GC])
        aftok = sb(hs, "aftok", [P, TB, GC])
        abtok = sb(hs, "abtok", [P, TB, GC])
        vtok = sb(hs, "vtok", [P, TB, GC])
        sz = sb(hs, "sz", [P, TB, GC])
        qT = sb(hs, "qT", [P, HPG, S])
        kf = sb(hs, "kf", [P, HPG, S])
        kb = sb(hs, "kb", [P, HPG, S])
        Bc = sb(hs, "Bc", [P, HPG, S])
        Xc = sb(hs, "Xc", [P, HPG, S])
        E = sb(hs, "E", [P, 2, 2, HPG, S])
        ST = sb(hs, "ST", [P, 2, HPG, 2, P])
        ssh = sb(hs, "ssh", [P, 3, 2 * HPG])
        hs.close()
        yl2 = ExitStack()
        hy_lo = sb(yl2, "hy_lo", [P, KT, S], F32R)
        apad = sb(yl2, "apad", [P, 5, TB, GC])
        kvtok = sb(yl2, "kvtok", [P, TB, GC])
        aq = sb(yl2, "aq", [P, TB, GC])
        asq = apad[:, 0, :, :]
        ar = apad[:, 1, :, :]
        ay = apad[:, 2, :, :]
        kdup = apad[:, 3, :, :].rearrange("p a (b c d) -> p a b c d", b=KVH, c=2)
        kT = sb(yl2, "kT", [P, KVH, S])
        aqT = sb(yl2, "aqT", [P, 4, S])
        sm = sb(yl2, "sm", [P, 8, 3 * P])
        PT = sb(yl2, "PT", [P, 2, 3 * P])
        rot = sb(yl2, "rot", [P, 2, 4, TB, HD // 2])
        ang = sb(yl2, "ang", [P, 3, TB, HD // 2])
        posf = sb(yl2, "posf", [P, TB])
        ast = sb(yl2, "ast", [P, 9, 16])
        yl2.close()
        mix.close()
        f_hi = sb(ctx, "f_hi", [P, FKT, S], F32R)
        f_lo = sb(ctx, "f_lo", [P, FKT, S], F32R)

        acc = ctx.enter_context(nc.psum_tensor("acc", [P, 2, TB, GC], F32))
        T = ctx.enter_context(nc.psum_tensor("T", [P, 4, 512], F32))
        T01 = T[:, 0:2, :]
        T23 = T[:, 2:4, :]

        raw_in = [sem(f"raw_in{s}") for s in range(SLOTS)]
        hi_ready, split_ready, chunk_used = sem("hi_ready"), sem("split_ready"), sem("chunk_used")
        pair_free = [sem("pair_free0"), sem("pair_free1")]
        small_in, table_in, x_in = sem("small_in"), sem("table_in"), [sem(f"x_in{k}") for k in range(4)]
        const_ready, feat_T, feat_ready = sem("const_ready"), sem("feat_T"), sem("feat_ready")
        lb_diff, lb_ready = sem("lb_diff"), sem("lb_ready")
        x_done = sem("x_done")
        n_sq, n_ms, n_std, n_rstd, n_T, n_hi, n_lo = (sem(f"norm_{s}") for s in ("sq", "ms", "std", "rstd", "T", "hi", "lo"))
        c_a, c_sg, c_v, c_T, c_pad, c_tap = (sem(f"conv_{s}") for s in ("a", "sg", "v", "T", "pad", "tap"))
        c_diag, c_sums = sem("conv_diag"), sem("conv_sums")
        c_z, c_zT, c_zc, c_mean, c_d, c_sq, c_var, c_std, c_n, c_act, c_g, c_hi, c_lo = (
            sem(f"ln_{s}") for s in ("z", "zT", "zc", "mean", "d", "sq", "var", "std", "n", "act", "g", "hi", "lo"))
        g_raw, g_T, g_act, g_aff, g_D, g_E, g_G, g_mm, g_S = (
            sem(f"hgrn_{s}") for s in ("raw", "T", "act", "aff", "D", "E", "G", "mm", "S"))
        g_av, g_o, g_ss, g_std, g_on, g_z, g_y, g_yT, g_hi, g_lo = (
            sem(f"hgrn_{s}") for s in ("av", "o", "ss", "std", "on", "z", "y", "yT", "yhi", "ylo"))
        a_cs, a_ang, a_ev, a_sq, a_ss, a_std, a_rp, a_T, a_cp = (
            sem(f"att_{s}") for s in ("cs", "ang", "ev", "sq", "ss", "std", "rope", "T", "cp"))
        a_s, a_sm, a_m, a_p, a_sink, a_pt, a_ptc, a_o, a_y, a_yT, a_hi, a_lo = (
            sem(f"att_{s}") for s in ("s", "sm", "m", "p", "sink", "pt", "ptc", "o", "y", "yT", "yhi", "ylo"))
        f_g, f_y, f_T, f_h, f_l = (sem(f"ffn_{s}") for s in ("g", "y", "T", "hi", "lo"))
        out_ready, out_done = sem("out_ready"), sem("out_done")

        def rounded(ap):
            return ap.bitcast(F32)

        def flat(ap):
            return ap.rearrange("p a b -> p (a b)")

        def group_columns(k):
            return slice(k * GC, (k + 1) * GC)

        def slots(base, i):
            return base + i, i % SLOTS, base * (16 // SLOTS) + 16 * (i // SLOTS + 1)

        block = ctx.enter_context(nc.Block())

        @block.sync
        def _(sp):
            for k in range(4):
                sp.dma_start(x[:, :, group_columns(k)], t["x"].rearrange("a (b p) d -> p (a b) d", p=P)[:, :, group_columns(k)]
                             ).then_inc(x_in[k], 16)

            def stream(name, j, source):
                base = ph[name].base(j)
                for i, (k, c) in enumerate(ph[name].seq):
                    n, slot, _ = slots(base, i)
                    W, col = source(k)
                    if not (isinstance(n, int) and n < SLOTS):
                        sp.wait_ge(split_ready, n - SLOTS + 1)
                    sp.dma_start(raw[:, slot, :, :], W[c * CK * P:(c + 1) * CK * P, bass.ds(col, GC)]
                                 .rearrange("(k p) n -> p k n", p=P)).then_inc(raw_in[slot], 16)

            W = t["conv_w_in"][0]
            ab = lambda j: stream("conv_ab", j, lambda k: (W, k * D + j * GC))
            ab(0)
            with sp.Fori(1, 4) as j:
                ab(j)
            stream("conv_z", 0, lambda k: (W, 2 * D + k * GC))
            stream("conv_out", 0, lambda k: (t["conv_w_out"][0], k * GC))
            with sp.Fori(0, 4) as j:
                stream("hgrn", j, lambda k: (t["hgrn_w_in"][0], k * D + j * GC))
            stream("hgrn_z", 0, lambda k: (t["hgrn_w_in"][0], 4 * D + k * GC))
            stream("hgrn_out", 0, lambda k: (t["hgrn_w_out"][0], k * GC))
            stream("kv_q", 0, lambda k: (t["attn_w_qkv_2"][0], (k - 1) * GC if k else D))
            stream("att_out", 0, lambda k: (t["attn_w_o_2"][0], k * GC))
            with sp.Fori(0, FJ) as j:
                stream("gate_up", j, lambda k: (t[("ffn_w_gate_2", "ffn_w_up_2")[k]][0], j * GC))
            stream("down", 0, lambda k: (t["ffn_w_down_2"][0], k * GC))
            for k in range(4):
                sp.wait_ge(out_ready, k + 1)
                sp.dma_start(out.rearrange("a (b p) d -> p (a b) d", p=P)[:, :, group_columns(k)],
                             x[:, :, group_columns(k)]).then_inc(out_done, 16)
            sp.wait_ge(out_done, 64)

        @block.gpsimd
        def _(pool):
            nc.gpsimd.memset(eps[:, :], EPS).then_inc(const_ready, 1)
            nc.gpsimd.memset(ones[:, :], 1.0 / D).then_inc(const_ready, 1)
            nc.gpsimd.memset(vpad[:, :, :], 0.0).then_inc(const_ready, 1)

        @block.tensor
        def _(pe):
            def transposes(dst, src, done):
                for q in range(4):
                    for tb in range(TB):
                        at = (q % 2) * S + tb * P
                        last = nc.tensor.transpose(dst[:, q // 2, at:at + P], src[:, tb, q * P:(q + 1) * P], ident[:, :])
                last.then_inc(done, 1)

            def stream(name, j, hi, lo, hooks=None, need=None):
                p = ph[name]
                base = p.base(j)
                for i, (k, c) in enumerate(p.seq):
                    n, slot, _ = slots(base, i)
                    if need is not None and k == 0:
                        need(c)
                    if c == 0 and not (isinstance(p.use(j, k), int) and p.use(j, k) == 0):
                        pe.wait_ge(pair_free[p.pair(k)], 2 * p.use(j, k))
                    pe.wait_ge(split_ready, n + 1)
                    for kk in range(CK):
                        for tb in range(TB):
                            kt = c * CK + kk
                            o, a = acc[:, p.pair(k), tb, :], slice(tb * P, (tb + 1) * P)
                            nc.tensor.matmul(o, hi[:, kt, a], w_hi[:, slot, kk, :], start=kt == 0, stop=False)
                            nc.tensor.matmul(o, hi[:, kt, a], w_lo[:, slot, kk, :], start=False, stop=False)
                            last = nc.tensor.matmul(o, lo[:, kt, a], w_hi[:, slot, kk, :], start=False,
                                                    stop=kt == p.chunks * CK - 1)
                    last.then_inc(chunk_used, 1)
                    for f in (hooks or {}).get(i, ()):
                        f()

            def x_turn(s, k, free=None):
                if s == 0:
                    pe.wait_ge(x_in[k], 16)
                else:
                    pe.wait_ge(x_done, 4 * (s - 1) + k + 1)
                if k and s:
                    pe.wait_ge(n_lo, 4 * s + k)
                elif k > 1:
                    pe.wait_ge(n_lo, k - 1)
                if free is not None:
                    pe.wait_ge(*free)
                transposes(T23 if s == 0 and k % 2 else T01, x[:, :, group_columns(k)], n_T)

            def x_turns(name, s, free):
                at = Hooks()
                for k in range(4):
                    at.put(ph[name].end(k) + (4 if ph[name].last[k] == ph[name].last.get(0, 0) + 2 else 2),
                           lambda k=k: x_turn(s, k, free if k == 0 else None))
                return at

            def normed(s):
                return lambda c: pe.wait_ge(n_lo, 4 * s + c // 2 + 1)

            pe.wait_ge(small_in, 16 * 11)
            for kt in range(KT):
                last = nc.tensor.transpose(T[:, 2 + kt // 8, (kt % 8) * ROWS:(kt % 8 + 1) * ROWS],
                                           rows[:, kt * P:(kt + 1) * P], ident[0:ROWS, 0:ROWS])
            last.then_inc(feat_T, 1)

            x_turn(0, 0)
            pe.wait_ge(feat_ready, 2)
            x_turn(0, 1)

            def v_turn(j):
                pe.wait_ge(c_v, j + 1)
                if not is_first(j):
                    pe.wait_ge(c_pad, 2 * j)
                transposes(T01, atok, c_T)

            def tap_sum(j, q):
                if q == 0:
                    pe.wait_ge(c_pad, 2 * (j + 1))
                    if not is_first(j):
                        pe.wait_ge(c_tap, 4 * STEPS * (j - 1) + 4 * (ADD_STEP + 1))
                pe.wait_ge(c_diag, 4 * j + q + 1)
                o = T[:, 2 + q // 2, (q % 2) * S:(q % 2 + 1) * S]
                for i in range(PE_TAPS):
                    tap = DVE_TAPS + i
                    last = nc.tensor.matmul(o, diag[:, q % 2, i, :], flat(vpad[:, bass.ds(4 * j + q, 1), tap:tap + S]),
                                            start=i == 0, stop=i == PE_TAPS - 1)
                last.then_inc(c_sums, 1)

            def tap_sums(j):
                at = Hooks()
                for q in range(4):
                    at.put(8 + 2 * q, lambda q=q: tap_sum(j, q))
                return at

            def ab(j):
                if is_first(j):
                    stream("conv_ab", j, h_hi, h_lo, Hooks().put(0, lambda: x_turn(0, 2)).put(1, lambda: x_turn(0, 3)), normed(0))
                else:
                    stream("conv_ab", j, h_hi, h_lo, tap_sums(j - 1).put(4, lambda: v_turn(j - 1)))
            ab(0)
            ab(1)
            with pe.Fori(2, 4) as j:
                ab(j)

            def z_turn(k):
                pe.wait_ge(c_z, k + 1)
                if k == 0:
                    pe.wait_ge(c_pad, 8)
                else:
                    pe.wait_ge(c_zc, 2 * k)
                transposes(T01, sg, c_zT)

            def mean(j):
                pe.wait_ge(c_tap, 4 * STEPS * (j + 1) if j == 3 else 4 * (3 * STEPS + ADD_STEP + 1))
                for kt in range(4 * j, 4 * j + 4):
                    last = nc.tensor.matmul(T[:, 2, 0:S], ones[:, :], cy[:, kt, :], start=kt == 0, stop=kt == KT - 1)
                if j == 3:
                    last.then_inc(c_mean, 1)

            def variance():
                for q in range(4):
                    pe.wait_ge(c_sq, q + 1)
                    for i in range(4):
                        last = nc.tensor.matmul(T[:, 3, 0:S], ones[:, :],
                                                (atok, sg)[q % 2].rearrange("p a (b c) -> p (a b) c", c=S)[:, i, :],
                                                start=q == 0 and i == 0, stop=q == 3 and i == 3)
                    last.then_inc(c_var, 1)
            at = tap_sums(3).put(4, lambda: v_turn(3)).put(25, lambda: mean(0)).put(26, lambda: mean(1)).put(27, lambda: mean(2))
            for k in range(3):
                at.put(8 * k + 12, lambda k=k: z_turn(k))
            stream("conv_z", 0, h_hi, h_lo, at)
            z_turn(3)
            mean(3)
            variance()
            stream("conv_out", 0, y_hi, y_lo, x_turns("conv_out", 1, (c_zc, 8)), lambda c: pe.wait_ge(c_lo, c // 2 + 1))

            def turn(j, i, src):
                pe.wait_ge(g_raw, 4 * j + i + 1)
                if i == 2:
                    pe.wait_ge(g_act, 5 * j + 1)
                elif i == 0 and not is_first(j):
                    pe.wait_ge(g_o, 2 * j)
                transposes(T23 if i == 1 else T01, src, g_T)

            def level(j, l):
                pe.wait_ge(g_G, 9 * j + l + 1)
                if l:
                    pe.wait_ge(g_S, 9 * j + l)
                e = E[:, l % 2, :, :, :]
                for h in range(HPG):
                    for b in range(2):
                        o = T[:, h // 2, (h % 2) * S + b * P:(h % 2) * S + b * P + P]
                        sl = slice(b * P, (b + 1) * P)
                        tl = slice((1 - b) * P, (2 - b) * P) if l == 0 else sl
                        q = qT[:, h, tl] if l == 1 else e[:, 1, h, tl]
                        last = nc.tensor.matmul(o, e[:, 0, h, sl], q, start=True, stop=True)
                last.then_inc(g_mm, 1)

            def av(j):
                pe.wait_ge(g_S, 9 * j + 9)
                for h in range(HPG):
                    v = lambda s: vtok[:, s, h * P:(h + 1) * P]
                    for tb in range(TB):
                        o = T[:, tb, h * P:(h + 1) * P]
                        nc.tensor.matmul(o, ST[:, 1, h, tb, :], v(tb), start=True, stop=False)
                        last = nc.tensor.matmul(o, ST[:, 0, h, 1 - tb, :], v(1 - tb), start=False, stop=True)
                last.then_inc(g_av, 1)

            def process(j):
                at = Hooks().put(0, lambda: turn(j, 0, qtok)).put(1, lambda: turn(j, 1, aftok)).put(3, lambda: turn(j, 2, abtok))
                for l in range(9):
                    at.put(10 + 2 * l, lambda l=l: level(j, l))
                return at.put(28, lambda: av(j))

            def qaai(j):
                if is_first(j):
                    stream("hgrn", j, h_hi, h_lo, x_turns("conv_out", 1, None).later(32), normed(1))
                else:
                    stream("hgrn", j, h_hi, h_lo, process(j - 1))
            qaai(0)
            qaai(1)
            with pe.Fori(2, 4) as j:
                qaai(j)

            def gated_turn(k):
                pe.wait_ge(g_y, k + 1)
                if k:
                    pe.wait_ge(g_lo, 2 * k)
                transposes(T23, sz, g_yT)
            at = process(3)
            for k in range(4):
                at.put(8 * k + 11, lambda k=k: gated_turn(k))
            stream("hgrn_z", 0, h_hi, h_lo, at)
            stream("hgrn_out", 0, y_hi, hy_lo, at.later(32).with_(x_turns("hgrn_out", 2, (g_o, 8))),
                   lambda c: pe.wait_ge(g_lo, 2 * (c // 2 + 1)))

            def k_turn():
                pe.wait_ge(a_rp, 1)
                for h in range(KVH):
                    for tb in range(TB):
                        last = nc.tensor.transpose(T[:, h // 2, (h % 2) * S + tb * P:(h % 2) * S + tb * P + P],
                                                   kdup[:, tb, h, :, :].rearrange("p a b -> p (a b)"), ident[:, :])
                last.then_inc(a_T, 1)

            def q_turn(g):
                pe.wait_ge(a_rp, g + 2)
                pe.wait_ge(a_cp, 2)
                if g:
                    pe.wait_ge(a_ptc, 8 * g)
                transposes(T01, ar, a_T)

            def scores(g, half):
                pe.wait_ge(a_cp, 2 * (g + 2))
                if half:
                    pe.wait_ge(a_sm, 8 * g + 4)
                elif g:
                    pe.wait_ge(a_lo, 2 * g)
                for h in range(4 * half, 4 * half + 4):
                    r = slice(HD * (h % 2), HD * (h % 2) + HD)
                    nc.tensor.matmul(T[:, h % 4, 0:P], aqT[r, h // 2, 0:P], kT[r, g, 0:P], start=True, stop=True)
                    nc.tensor.matmul(T[:, h % 4, P:3 * P], aqT[r, h // 2, P:S], kT[r, g, :], start=True,
                                     stop=True).then_inc(a_s, 1)

            def turn_p(g, i):
                for h in (2 * i, 2 * i + 1):
                    pe.wait_ge(a_p, 8 * g + h + 1)
                    if 8 * g + h >= 2:
                        pe.wait_ge(a_ptc, 8 * g + h - 1)
                    if h < 2:
                        pe.wait_ge(a_sm, 8 * g + 8)
                    for b in range(3):
                        last = nc.tensor.transpose(T[:, h % 2, b * P:(b + 1) * P], sm[:, h, b * P:(b + 1) * P], ident[:, :])
                    last.then_inc(a_pt, 1)

            def mix_v(g, i):
                for h in (2 * i, 2 * i + 1):
                    pe.wait_ge(a_ptc, 8 * g + h + 1)
                    v = lambda tb: kvtok[:, tb, S + g * HD:S + (g + 1) * HD]
                    o = lambda tb: T[:, 2 + tb, h * HD:(h + 1) * HD]
                    nc.tensor.matmul(o(0), PT[:, h % 2, 0:P], v(0), start=True, stop=True)
                    nc.tensor.matmul(o(1), PT[:, h % 2, P:2 * P], v(0), start=True, stop=False)
                    nc.tensor.matmul(o(1), PT[:, h % 2, 2 * P:3 * P], v(1), start=False, stop=True).then_inc(a_o, 1)

            def y_turn(g):
                pe.wait_ge(a_y, g + 1)
                transposes(T23, ay, a_yT)

            at = Hooks().put(14, k_turn)
            for g in range(4):
                e = 16 + 8 * g
                at.put(e + 6, lambda g=g: q_turn(g))
                if g:
                    at.put(e + 7, lambda g=g: y_turn(g - 1))
                at.put(e + 8, lambda g=g: scores(g, 0)).put(e + 9, lambda g=g: scores(g, 1))
                for i in range(4):
                    at.put(e + 10 + i if g < 3 else e + 10, lambda g=g, i=i: turn_p(g, i))
                    at.put(e + 11 + i if g < 3 else e + 10, lambda g=g, i=i: mix_v(g, i))
            at.put(51, lambda: y_turn(3))
            stream("kv_q", 0, h_hi, h_lo, x_turns("hgrn_out", 2, None).later(32).with_(at), normed(2))
            early = at.later(40)
            stream("att_out", 0, y_hi, hy_lo, early.with_(x_turns("att_out", 3, (a_lo, 8))), lambda c: pe.wait_ge(a_lo, 2 * (c // 2 + 1)))

            def f_turn(j):
                pe.wait_ge(f_y, j + 1)
                if not is_first(j):
                    pe.wait_ge(f_l, 2 * j)
                transposes(T01, fg, f_T)

            def gu(j):
                if is_first(j):
                    stream("gate_up", j, h_hi, h_lo, x_turns("att_out", 3, None).later(32), normed(3))
                else:
                    stream("gate_up", j, h_hi, h_lo, Hooks().put(3, lambda: f_turn(j - 1)))
            gu(0)
            gu(1)
            with pe.Fori(2, FJ) as j:
                gu(j)
            stream("down", 0, f_hi, f_lo, Hooks().put(3, lambda: f_turn(FJ - 1)),
                   lambda c: pe.wait_ge(f_l, 2 * (c // 2 + 1)))

        @block.scalar
        def _(act):
            A = nc.scalar.activation

            for dst, src in ((ident[:, :], t["c_ident"]), (rows[R_NORM0:R_NORM0 + 1, :], t["conv_norm"]),
                             (rows[0:TAPS, :], t["conv_dw"][0]), (rows[R_DWB:R_DWB + 1, :], t["conv_dw_b"]),
                             (rows[R_LNG:R_LNG + 1, :], t["conv_ln_g"]), (rows[R_LNB:R_LNB + 1, :], t["conv_ln_b"]),
                             (rows[R_NORM1:R_NORM1 + 1, :], t["hgrn_norm"]),
                             (rows[R_NORM2:R_NORM2 + 1, :], t["mixer_norm_2"]), (rows[R_NORM3:R_NORM3 + 1, :], t["ffn_norm_2"]),
                             (rows[R_F0:R_F0 + 2, :], t["hgrn_lb_fwd"]), (rows[R_B0:R_B0 + 2, :], t["hgrn_lb_bwd"])):
                act.dma_start(dst, src).then_inc(small_in, 16)

            def tables():
                for dst, src in ((lmask[:, :, :], t["c_lmask"]), (wmask[:, :], t["c_wmask"]),
                                 (inv_freq[:, :], t["c_inv_freq"][0].partition_broadcast(P)),
                                 (onorm[:, :], t["hgrn_o_norm"][0].partition_broadcast(P)),
                                 (qkn[:, 0, :], t["attn_q_norm_2"][0].partition_broadcast(P)),
                                 (qkn[:, 1, :], t["attn_k_norm_2"][0].partition_broadcast(P)),
                                 (sinks[:, :], t["attn_sinks_2"][0].partition_broadcast(P)),
                                 (posi[:, :], t["positions_2"].rearrange("a (b p) -> p (a b)", p=P))):
                    act.dma_start(dst, src, allow_slow_non_contiguous=True).then_inc(table_in, 16)

            def stream(name, j, hooks=None):
                base = ph[name].base(j)
                for i in range(len(ph[name].seq)):
                    n, slot, loads = slots(base, i)
                    act.wait_ge(raw_in[slot], loads)
                    if not (isinstance(n, int) and n < SLOTS):
                        act.wait_ge(chunk_used, n - SLOTS + 1)
                    A(w_hi[:, slot, :, :], raw[:, slot, :, :], ACT.Copy).then_inc(hi_ready, 1)
                    for f in (hooks or {}).get(i, ()):
                        f()

            def evacuate(name, j, k, norm, dst, func=ACT.Copy, done=None):
                act.wait_ge(n_rstd, norm + 1)
                act.wait_ge(chunk_used, ph[name].done(j, k))
                for tb in range(TB):
                    A(dst[:, tb, :], acc[:, ph[name].pair(k), tb, :], func, scale=rs[:, norm, tb:tb + 1]).then_inc(pair_free[ph[name].pair(k)], 1)
                nc.scalar.drain().then_inc(done, 1)

            def x_hi(s, k):
                act.wait_ge(n_T, 4 * s + k + 1)
                bank = 2 * (k % 2) if s == 0 else 0
                for q in range(4):
                    kt = 4 * k + q
                    last = A(h_hi[:, kt, :], T[:, bank + q // 2, (q % 2) * S:(q % 2 + 1) * S], ACT.Copy,
                             scale=feat[:, kt, R_NORM0 + s:R_NORM0 + s + 1])
                last.then_inc(n_hi, 1)

            def x_squares(s, k):
                if s == 0:
                    act.wait_ge(x_in[k], 16)
                else:
                    act.wait_ge(x_done, 4 * (s - 1) + k + 1)
                nc.scalar.drain()
                for tb in range(TB):
                    last = A(fg[:, tb, :], x[:, tb, group_columns(k)], ACT.Square, accum_out=ssq[:, tb, k:k + 1])
                last.then_inc(n_sq, 1)

            def x_std(s):
                if s == 0:
                    act.wait_ge(const_ready, 3)
                act.wait_ge(n_ms, s + 1)
                A(rms[:, 1, :], rms[:, 0, :], ACT.Sqrt, scale=1.0 / D, bias=eps[:, 0:1]).then_inc(n_std, 1)

            def x_norm(name, s):
                at = Hooks()
                for k in range(4):
                    e = ph[name].end(k)
                    at.put(e + 3, lambda k=k: x_squares(s, k)).put(e + 4, lambda k=k: x_hi(s, k))
                return at.put(ph[name].end(3) + 5, lambda: x_std(s))

            act.wait_ge(feat_T, 1)
            for b in range(2):
                A(feat[:, 8 * b:8 * b + 8, :].rearrange("p a b -> p (a b)"), T[:, 2 + b, 0:8 * ROWS], ACT.Copy).then_inc(feat_ready, 1)
            act.wait_ge(feat_ready, 2)

            def bounds_out():
                act.wait_ge(lb_diff, 2)
                for d in range(2):
                    A(lbt[:, d, 1, :], lbt[:, d, 0, :], ACT.Sigmoid, scale=-1.0)
                    A(lbt[:, d, 0, :], lbt[:, d, 0, :], ACT.Sigmoid).then_inc(lb_ready, 1)

            def pad_copy(j):
                act.wait_ge(c_T, j + 1)
                for b in range(2):
                    A(vpad[:, bass.ds(4 * j + 2 * b, 2), PAD:PAD + S], T[:, b, :].rearrange("p (a b) -> p a b", a=2),
                      ACT.Copy).then_inc(c_pad, 1)

            def diagonals(j, q):
                if q >= 2 or not is_first(j):
                    act.wait_ge(c_sums, 4 * j + q - 1)
                for i in range(PE_TAPS):
                    last = A(diag[:, q % 2, i, :], ident[:, :], ACT.Copy,
                             scale=flat(feat[:, bass.ds(4 * j + q, 1), DVE_TAPS + i:DVE_TAPS + i + 1]))
                last.then_inc(c_diag, 1)

            def v_steps(j):
                at = Hooks().put(2, lambda: b_out(j)).put(6, lambda: pad_copy(j))
                for q, tick in enumerate((4, 7, 10, 12)):
                    at.put(tick, lambda q=q: diagonals(j, q))
                return at

            def a_out(j):
                if not is_first(j):
                    act.wait_ge(c_T, j)
                evacuate("conv_ab", j, 0, 0, atok, ACT.Copy, c_a)

            def b_out(j):
                evacuate("conv_ab", j, 1, 0, sg, ACT.Sigmoid, c_sg)

            def ab(j):
                at = Hooks()
                if is_first(j):
                    for k in range(4):
                        at.put(k, lambda k=k: x_hi(0, k)).put(4 + k // 2, lambda k=k: x_squares(0, k))
                    at.put(6, lambda: x_std(0)).put(7, tables).put(12, bounds_out)
                else:
                    at = v_steps(j - 1)
                stream("conv_ab", j, at.put(10, lambda: a_out(j)))
            ab(0)
            ab(1)
            with act.Fori(2, 4) as j:
                ab(j)

            def z_out(k):
                if k:
                    act.wait_ge(c_zT, k)
                evacuate("conv_z", 0, k, 0, sg, ACT.Silu, c_z)

            def z_copy(k):
                act.wait_ge(c_zT, k + 1)
                for b in range(2):
                    A(szt[:, 4 * k + 2 * b:4 * k + 2 * b + 2, :].rearrange("p a b -> p (a b)"), T[:, b, :],
                      ACT.Copy).then_inc(c_zc, 1)
            at = v_steps(3)
            for k in range(3):
                at.put(8 * k + 10, lambda k=k: z_out(k)).put(8 * k + 15, lambda k=k: z_copy(k))
            stream("conv_z", 0, at)

            def layer_norm():
                z_out(3)
                z_copy(3)
                for q in range(4):
                    act.wait_ge(c_d, q + 1)
                    if q >= 2:
                        act.wait_ge(c_var, q - 1)
                    A(flat((atok, sg)[q % 2]), flat(cy[:, 4 * q:4 * q + 4, :]), ACT.Square).then_inc(c_sq, 1)
                act.wait_ge(c_var, 4)
                A(ln_std[:, :], T[:, 3, 0:S], ACT.Sqrt, bias=eps[:, 0:1]).then_inc(c_std, 1)
                for q in range(2):
                    ln_act(q)
                ln_hi(0)

            def ln_act(q):
                act.wait_ge(c_n, q + 1)
                for kt in range(4 * q, 4 * q + 4):
                    last = A(cy[:, kt, :], cy[:, kt, :], ACT.Silu, scale=feat[:, kt, R_LNG:R_LNG + 1], bias=feat[:, kt, R_LNB:R_LNB + 1])
                last.then_inc(c_act, 1)

            def ln_hi(q):
                act.wait_ge(c_g, q + 1)
                A(y_hi[:, 4 * q:4 * q + 4, :], cy[:, 4 * q:4 * q + 4, :], ACT.Copy).then_inc(c_hi, 1)
            at = Hooks().put(3, layer_norm).put(4, lambda: ln_hi(1)).put(4, lambda: ln_act(2)).put(5, lambda: ln_hi(2))
            at.put(5, lambda: ln_act(3)).put(6, lambda: ln_hi(3))
            stream("conv_out", 0, at.with_(x_norm("conv_out", 1)))

            def raw_out(j, k, dst):
                if not is_first(j):
                    if k < 3:
                        act.wait_ge(g_T, 3 * (j - 1) + k + 1)
                    else:
                        act.wait_ge(g_av, j)
                evacuate("hgrn", j, k, 1, dst, ACT.Copy, g_raw)

            def q_copy(j):
                act.wait_ge(g_T, 3 * j + 1)
                if not is_first(j):
                    act.wait_ge(g_mm, 9 * j)
                A(flat(qT[:, :, :]), flat(T01), ACT.Copy).then_inc(g_act, 1)

            def gates(j, d):
                act.wait_ge(g_T, 3 * j + 2 + d)
                if not is_first(j):
                    act.wait_ge(g_on, j)
                s = Bc[:, :, :] if d == 0 else E[:, 1, 0, :, :]
                a = (T23, T01)[d]
                A(flat(s), flat(a), ACT.Sigmoid)
                A(flat((kf, kb)[d][:, :, :]), flat(a), ACT.Sigmoid, scale=-1.0).then_inc(g_act, 1)

            def ln(j, d):
                act.wait_ge(g_aff, 2 * j + d + 1)
                s = Bc[:, :, :] if d == 0 else E[:, 1, 0, :, :]
                A(flat(s), flat(s), ACT.Ln).then_inc(g_act, 1)

            def exp(j, l):
                act.wait_ge(g_D, 8 * j + max(l, 1))
                e = E[:, l % 2, :, :, :].rearrange("p a b c -> p (a b c)")
                A(e, e, ACT.Exp).then_inc(g_E, 1)

            def take(j, l):
                act.wait_ge(g_mm, 9 * j + l + 1)
                if l == 0 and not is_first(j):
                    act.wait_ge(g_av, j)
                A(ST[:, l, :, :, :].rearrange("p a b c -> p (a b c)"), flat(T01), ACT.Copy).then_inc(g_S, 1)

            def o_out(j):
                act.wait_ge(g_av, j + 1)
                A(flat(E[:, 1, 0, :, :]), flat(T01), ACT.Copy).then_inc(g_o, 1)
                A(flat(E[:, 1, 1, :, :]), flat(T01), ACT.Square).then_inc(g_o, 1)

            def o_std(j):
                act.wait_ge(g_ss, j + 1)
                A(ssh[:, 1, :], ssh[:, 0, :], ACT.Sqrt, scale=1.0 / P, bias=eps[:, 0:1]).then_inc(g_std, 1)

            def process(j):
                at = Hooks().put(3, lambda: q_copy(j)).put(4, lambda: gates(j, 0)).put(6, lambda: gates(j, 1))
                at.put(6, lambda: ln(j, 0)).put(8, lambda: ln(j, 1)).put(10, lambda: exp(j, 0))
                for l in range(2):
                    at.put(13 + 2 * l, lambda l=l: take(j, l))
                for l in range(2, 9):
                    at.put(11 + 2 * l, lambda l=l: exp(j, l))
                return at.put(30, lambda: o_out(j)).put(31, lambda: o_std(j))

            def qaai(j):
                at = x_norm("conv_out", 1).later(32) if is_first(j) else Hooks().put(0, lambda: raw_out(j - 1, 3, vtok)).with_(process(j - 1))
                for k, dst in enumerate((qtok, aftok, abtok)):
                    at.put(8 * k + 10, lambda k=k, dst=dst: raw_out(j, k, dst))
                stream("hgrn", j, at)
            qaai(0)
            qaai(1)
            with act.Fori(2, 4) as j:
                qaai(j)

            def hz_out(k):
                if k:
                    act.wait_ge(g_yT, k)
                evacuate("hgrn_z", 0, k, 1, sz, ACT.Silu, g_z)

            def hz_hi(k):
                act.wait_ge(g_yT, k + 1)
                for b in range(2):
                    A(flat(y_hi[:, 4 * k + 2 * b:4 * k + 2 * b + 2, :]), T[:, 2 + b, :], ACT.Copy).then_inc(g_hi, 1)
            at = Hooks().put(0, lambda: raw_out(3, 3, vtok)).with_(process(3))
            for k in range(4):
                at.put(8 * k + 10, lambda k=k: hz_out(k)).put(8 * k + 13, lambda k=k: hz_hi(k))
            stream("hgrn_z", 0, at)

            def sines():
                act.wait_ge(a_ang, 1)
                A(cs[:, 0, :, :].rearrange("p a b -> p (a b)"), ang[:, 0, :, :].rearrange("p a b -> p (a b)"), ACT.Sin)
                A(cs[:, 1, :, :].rearrange("p a b -> p (a b)"), ang[:, 1, :, :].rearrange("p a b -> p (a b)"), ACT.Sin).then_inc(a_cs, 1)
            stream("hgrn_out", 0, at.later(32).with_(x_norm("hgrn_out", 2)).put(16, sines))

            def q_out(g):
                if g >= 0:
                    act.wait_ge(a_rp, g + 1)
                src = kvtok if g < 0 else aq
                evacuate("kv_q", 0, g + 1, 2, src, ACT.Copy, a_ev)
                w = KVH * HD if g < 0 else GC
                A(asq[:, :, 0:w], src[:, :, 0:w], ACT.Square).then_inc(a_sq, 1)

            def q_std(g):
                act.wait_ge(a_ss, g + 2)
                w = 2 * KVH if g < 0 else 16
                A(ast[:, 1, 0:w], ast[:, 0, 0:w], ACT.Sqrt, scale=1.0 / HD, bias=eps[:, 0:1]).then_inc(a_std, 1)

            def qk_copy(g):
                act.wait_ge(a_T, g + 2)
                dst = kT if g < 0 else aqT
                for b in range(2):
                    A(flat(dst[:, 2 * b:2 * b + 2, :]), T[:, b, :], ACT.Copy).then_inc(a_cp, 1)

            def exps(g, h0, h1):
                act.wait_ge(a_m, g + 1)
                for h in range(h0, h1):
                    A(sm[:, h, 0:P], sm[:, h, 0:P], ACT.Exp, bias=ast[:, 2, h:h + 1], accum_out=ast[:, 4, h:h + 1])
                    A(sm[:, h, P:3 * P], sm[:, h, P:3 * P], ACT.Exp, bias=ast[:, 2, 8 + h:9 + h],
                      accum_out=ast[:, 4, 8 + h:9 + h]).then_inc(a_p, 1)
                if h1 == 8:
                    A(ast[:, 5, :], ast[:, 3, :], ACT.Exp)
                    nc.scalar.drain().then_inc(a_sink, 1)

            def p_copy(g, i):
                for h in (2 * i, 2 * i + 1):
                    act.wait_ge(a_pt, 8 * g + h + 1)
                    if 8 * g + h >= 2:
                        act.wait_ge(a_o, 8 * g + h - 1)
                    A(PT[:, h % 2, :], T[:, h % 2, 0:3 * P], ACT.Copy).then_inc(a_ptc, 1)

            def y_out_hi(g):
                act.wait_ge(a_yT, g + 1)
                for b in range(2):
                    A(flat(y_hi[:, 4 * g + 2 * b:4 * g + 2 * b + 2, :]), T[:, 2 + b, :], ACT.Copy).then_inc(a_hi, 1)
            at = Hooks()
            for g in range(-1, 4):
                e = 16 + 8 * g
                at.put(e + 2, lambda g=g: q_out(g)).put(e + 3, lambda g=g: q_std(g))
                if g > 0:
                    at.put(e + 7, lambda g=g: p_copy(g - 1, 2)).put(e + 8, lambda g=g: p_copy(g - 1, 3))
                at.put(e + 9, lambda g=g: qk_copy(g))
                if g > 0:
                    at.put(e + 10, lambda g=g: y_out_hi(g - 1))
                if 0 <= g < 3:
                    at.put(e + 12, lambda g=g: exps(g, 0, 3))
                    at.put(e + 13, lambda g=g: p_copy(g, 0)).put(e + 13, lambda g=g: exps(g, 3, 6))
                    at.put(e + 14, lambda g=g: p_copy(g, 1)).put(e + 14, lambda g=g: exps(g, 6, 8))
            at.put(52, lambda: exps(3, 0, 8))
            for i in range(4):
                at.put(53, lambda i=i: p_copy(3, i))
            at.put(54, lambda: y_out_hi(3))
            stream("kv_q", 0, x_norm("hgrn_out", 2).later(32).with_(at))
            stream("att_out", 0, at.later(40).with_(x_norm("att_out", 3)))

            def g_out(j):
                if not is_first(j):
                    act.wait_ge(f_T, j)
                evacuate("gate_up", j, 0, 3, fg, ACT.Silu, f_g)

            def f_hi_out(j):
                act.wait_ge(f_T, j + 1)
                for b in range(2):
                    A(f_hi[:, bass.ds(4 * j + 2 * b, 2), :], T[:, b, :].rearrange("p (a b) -> p a b", a=2),
                      ACT.Copy).then_inc(f_h, 1)

            def gu(j):
                at = x_norm("att_out", 3).later(32) if is_first(j) else Hooks().put(5, lambda: f_hi_out(j - 1))
                stream("gate_up", j, at.put(10, lambda: g_out(j)))
            gu(0)
            gu(1)
            with act.Fori(2, FJ) as j:
                gu(j)
            stream("down", 0, Hooks().put(5, lambda: f_hi_out(FJ - 1)))

        @block.vector
        def _(dve):
            V = nc.vector
            TT = nc.vector.tensor_tensor
            STT = nc.vector.scalar_tensor_tensor

            def settle():
                return nc.vector.drain()

            def stream(name, j, hooks=None):
                base = ph[name].base(j)
                for i in range(len(ph[name].seq)):
                    n, slot, _ = slots(base, i)
                    dve.wait_ge(hi_ready, n + 1)
                    TT(w_lo[:, slot, :, :], raw[:, slot, :, :], rounded(w_hi[:, slot, :, :]), ALU.subtract).then_inc(split_ready, 1)
                    for f in (hooks or {}).get(i, ()):
                        f()

            def low(dst, src, hi, done):
                TT(dst, src, rounded(hi), ALU.subtract).then_inc(done, 1)

            def x_lo(s, k):
                dve.wait_ge(n_hi, 4 * s + k + 1)
                bank = 2 * (k % 2) if s == 0 else 0
                for q in range(4):
                    kt = 4 * k + q
                    last = STT(out=h_lo[:, kt, :], in0=T[:, bank + q // 2, (q % 2) * S:(q % 2 + 1) * S],
                               scalar=feat[:, kt, R_NORM0 + s:R_NORM0 + s + 1], in1=rounded(h_hi[:, kt, :]),
                               op0=ALU.mult, op1=ALU.subtract)
                last.then_inc(n_lo, 1)

            def residual(name, k):
                dve.wait_ge(chunk_used, ph[name].done(0, k))
                for tb in range(TB):
                    TT(x[:, tb, group_columns(k)], acc[:, ph[name].pair(k), tb, :], x[:, tb, group_columns(k)],
                       ALU.add).then_inc(pair_free[ph[name].pair(k)], 1)
                settle().then_inc(out_ready if name == "down" else x_done, 1)

            def x_sums(s):
                dve.wait_ge(n_sq, 4 * (s + 1))
                V.tensor_reduce(rms[:, 0, :], ssq[:, :, :], AX.X, ALU.add).then_inc(n_ms, 1)

            def x_rstd(s):
                dve.wait_ge(n_std, s + 1)
                V.reciprocal(rs[:, s, :], rms[:, 1, :]).then_inc(n_rstd, 1)

            def x_norm(name, s):
                at = Hooks()
                for k in range(4):
                    e = ph[name].end(k)
                    at.put(e + 2, lambda k=k: residual(name, k)).put(e + 5, lambda k=k: x_lo(s, k))
                return at.put(ph[name].end(3) + 4, lambda: x_sums(s)).put(ph[name].end(3) + 6, lambda: x_rstd(s))

            def v_out(j):
                dve.wait_ge(c_a, j + 1)
                dve.wait_ge(c_sg, j + 1)
                TT(atok[:, :, :], atok[:, :, :], sg[:, :, :], ALU.mult).then_inc(c_v, 1)

            def taps(j, part, parts):
                n = 4 * STEPS
                for i in range(part * n // parts, (part + 1) * n // parts):
                    step, q = i // 4, i % 4
                    kt = bass.ds(4 * j + q, 1)
                    y = flat(cy[:, kt, :])
                    if i == 0:
                        dve.wait_ge(c_pad, 2 * (j + 1))
                    elif step:
                        dve.wait_ge(c_tap, j * n + i - 3)
                    if step == ADD_STEP:
                        dve.wait_ge(c_sums, 4 * j + 2 * (q // 2) + 2)
                        TT(y, y, T[:, 2 + q // 2, (q % 2) * S:(q % 2 + 1) * S], ALU.add).then_inc(c_tap, 1)
                        continue
                    tap = step - (step > ADD_STEP)
                    v = flat(vpad[:, kt, tap:tap + S])
                    w = flat(feat[:, kt, tap:tap + 1])
                    if step == 0:
                        V.tensor_scalar(y, v, w, flat(feat[:, kt, R_DWB:R_DWB + 1]), ALU.mult, ALU.add).then_inc(c_tap, 1)
                    else:
                        STT(out=y, in0=v, scalar=w, in1=y, op0=ALU.mult, op1=ALU.add).then_inc(c_tap, 1)

            def bounds_in():
                for d, (r0, r1) in enumerate(((R_F0, R_F1), (R_B0, R_B1))):
                    TT(lbt[:, d, 0, :], feat[:, :, r1], feat[:, :, r0], ALU.subtract).then_inc(lb_diff, 1)

            def ab(j, oldest):
                at = Hooks()
                if is_first(j):
                    for k in range(4):
                        at.put(k, lambda k=k: x_lo(0, k))
                    at.put(5, lambda: x_sums(0)).put(6, lambda: x_rstd(0)).put(8, bounds_in)
                else:
                    at.put(3, lambda: v_out(j - 1))
                    for c in range(8):
                        if not oldest:
                            at.put(c, lambda c=c: taps(j - 2, 8 + c, 16))
                        at.put(8 + c, lambda c=c: taps(j - 1, c, 16))
                stream("conv_ab", j, at)
            dve.wait_ge(feat_ready, 2)
            ab(0, False)
            ab(1, True)
            with dve.Fori(2, 4) as j:
                ab(j, False)
            at = Hooks().put(3, lambda: v_out(3))
            for c in range(8):
                at.put(c, lambda c=c: taps(2, 8 + c, 16))
            for c in range(24):
                at.put(8 + c, lambda c=c: taps(3, c, 24))
            stream("conv_z", 0, at)

            def block_of(q):
                return cy[:, 4 * q:4 * q + 4, :]

            def layer_norm():
                settle()
                dve.wait_ge(c_mean, 1)
                for q in range(4):
                    TT(block_of(q), block_of(q), T[:, 2, 0:S].unsqueeze(1).to_broadcast([P, 4, S]), ALU.subtract).then_inc(c_d, 1)
                dve.wait_ge(c_std, 1)
                V.reciprocal(ln_rstd[:, :], ln_std[:, :])
                settle()
                for q in range(4):
                    TT(block_of(q), block_of(q), ln_rstd[:, :].unsqueeze(1).to_broadcast([P, 4, S]), ALU.mult).then_inc(c_n, 1)
                    if q == 1:
                        ln_gate(0)
                ln_lo(0)
                ln_gate(1)

            def ln_gate(q):
                dve.wait_ge(c_zc, 8)
                dve.wait_ge(c_act, q + 1)
                TT(block_of(q), block_of(q), szt[:, 4 * q:4 * q + 4, :], ALU.mult).then_inc(c_g, 1)

            def ln_lo(q):
                dve.wait_ge(c_hi, q + 1)
                low(y_lo[:, 4 * q:4 * q + 4, :], block_of(q), y_hi[:, 4 * q:4 * q + 4, :], c_lo)
            at = Hooks().put(3, layer_norm).put(4, lambda: ln_lo(1)).put(4, lambda: ln_gate(2)).put(5, lambda: ln_lo(2))
            at.put(5, lambda: ln_gate(3)).put(6, lambda: ln_lo(3))
            stream("conv_out", 0, at.with_(x_norm("conv_out", 1)))

            dve.wait_ge(lb_ready, 2)
            dve.wait_ge(table_in, 16 * 8)

            def affine(j, d):
                dve.wait_ge(g_act, 5 * j + (2, 3)[d])
                k = (kf, kb)[d]
                s = Bc if d == 0 else E[:, 1, 0, :, :]
                for h in range(HPG):
                    lb = lbt[:, d, 0, bass.ds(4 * j + h, 1)]
                    ob = lbt[:, d, 1, bass.ds(4 * j + h, 1)]
                    V.tensor_scalar(s[:, h, :], s[:, h, :], ob, lb, ALU.mult, ALU.add)
                    V.tensor_scalar(k[:, h, :], k[:, h, :], ob, None, ALU.mult)
                settle()
                s = s[:, :, :].rearrange("p a b -> p (a b)")
                V.tensor_scalar(s, s, LN_MIN, None, ALU.max).then_inc(g_aff, 1)

            def scans(j):
                dve.wait_ge(g_act, 5 * j + 5)
                lf = E[:, 1, 0, :, :]
                for h in range(HPG):
                    V.tensor_tensor_scan(Bc[:, h, :], Bc[:, h, :], Bc[:, h, :], 0.0, ALU.add, ALU.bypass)
                    V.tensor_tensor_scan(Xc[:, h, 1:S], lf[:, h, 0:S - 1], lf[:, h, 0:S - 1], 0.0, ALU.add, ALU.bypass)
                V.memset(Xc[:, :, 0:1], 0.0)
                settle()

            def halves(a, c):
                v = a.rearrange("p h (b two c) -> p (h b) two c", two=2, c=c)
                return v[:, :, 0, :], v[:, :, 1, :]

            def bounds(c):
                n = HPG * S // (2 * c)
                f = halves(Bc[:, :, :], c)[0][:, :, c - 1:c]
                b = halves(Xc[:, :, :], c)[1][:, :, 0:1]
                return f.to_broadcast([P, n, c]), b.to_broadcast([P, n, c])

            def width(l):
                return P if l == 0 else LEVELS[l - 2]

            def diffs(j, l):
                e = E[:, l % 2, :, :, :]
                if l >= 2:
                    dve.wait_ge(g_mm, 9 * j + l - 1)
                if l == 1:
                    TT(e[:, 0, :, :], kf[:, :, :], kb[:, :, :], ALU.add)
                    return
                c = width(l)
                rf, rb = bounds(c)
                fl, fr = halves(Bc[:, :, :], c)
                bl, br = halves(Xc[:, :, :], c)
                gl, gr = halves(e[:, 0, :, :], c)
                ql, qr = halves(e[:, 1, :, :], c)
                TT(gl, rf, fl, ALU.subtract)
                TT(gr, br, rb, ALU.subtract)
                TT(ql, rb, bl, ALU.subtract)
                TT(qr, fr, rf, ALU.subtract).then_inc(g_D, 1)

            def weigh(j, l):
                if l == 1:
                    settle().then_inc(g_G, 1)
                    return
                e = E[:, l % 2, :, :, :]
                dve.wait_ge(g_E, 8 * j + max(l, 1))
                c = width(l)
                gl, gr = halves(e[:, 0, :, :], c)
                TT(gl, gl, halves(kf[:, :, :], c)[0], ALU.mult)
                TT(gr, gr, halves(kb[:, :, :], c)[1], ALU.mult)
                TT(e[:, 1, :, :], e[:, 1, :, :], qT[:, :, :], ALU.mult).then_inc(g_G, 1)

            def take(j, l):
                settle()
                dve.wait_ge(g_mm, 9 * j + l + 1)
                ps = flat(T01)
                V.memset(none[:, :], 0.0)
                V.copy_predicated(ST[:, 1, :, :, :].rearrange("p a b c -> p (a b) c"),
                                  lmask[:, l - 2, :].unsqueeze(1).to_broadcast([P, 8, P]),
                                  ps.rearrange("p (a c) -> p a c", c=P)).then_inc(g_S, 1)

            def o_norm(j):
                dve.wait_ge(g_o, 2 * (j + 1))
                V.tensor_reduce(ssh[:, 0, :], E[:, 1, 1, :, :].rearrange("p a (b c) -> p (a b) c", c=P), AX.X, ALU.add).then_inc(g_ss, 1)

            def o_scale(j):
                dve.wait_ge(g_std, j + 1)
                V.reciprocal(ssh[:, 2, :], ssh[:, 1, :])
                settle()
                e = E[:, 1, 0, :, :].rearrange("p a (b c) -> p (a b) c", c=P)
                TT(e, e, ssh[:, 2, :].unsqueeze(2).to_broadcast([P, 8, P]), ALU.mult)
                settle()
                TT(o_all[:, bass.ds(j, 1), :, :].rearrange("p z a (b c) -> p (z a b) c", c=P), e,
                   onorm[:, :].unsqueeze(1).to_broadcast([P, 8, P]), ALU.mult).then_inc(g_on, 1)

            def process(j):
                at = Hooks().put(5, lambda: affine(j, 0)).put(7, lambda: affine(j, 1)).put(9, lambda: scans(j)).put(9, lambda: diffs(j, 0))
                for l in range(9):
                    if l > 2:
                        at.put(11 + 2 * l, lambda l=l: take(j, l - 1))
                    at.put(11 + 2 * l, lambda l=l: weigh(j, l))
                    if l < 8:
                        at.put(11 + 2 * l, lambda l=l: diffs(j, l + 1))
                at.put(29, lambda: take(j, 8))
                return at.put(30, lambda: o_norm(j)).put(31, lambda: o_scale(j))

            def qaai(j):
                stream("hgrn", j, x_norm("conv_out", 1).later(32) if is_first(j) else process(j - 1))
            qaai(0)
            qaai(1)
            with dve.Fori(2, 4) as j:
                qaai(j)

            def gate(k):
                dve.wait_ge(g_on, k + 1)
                dve.wait_ge(g_z, k + 1)
                TT(sz[:, :, :], sz[:, :, :], o_all[:, k, :, :], ALU.mult).then_inc(g_y, 1)

            def z_lo(k):
                for b in range(2):
                    dve.wait_ge(g_hi, 2 * k + b + 1)
                    kk = slice(4 * k + 2 * b, 4 * k + 2 * b + 2)
                    low(flat(hy_lo[:, kk, :]), T[:, 2 + b, :], flat(y_hi[:, kk, :]), g_lo)
            at = process(3)
            for k in range(4):
                at.put(8 * k + 11, lambda k=k: gate(k)).put(8 * k + 14, lambda k=k: z_lo(k))
            stream("hgrn_z", 0, at)

            def angles():
                V.tensor_copy(posf[:, :], posi[:, :])
                settle()
                for tb in range(TB):
                    V.tensor_scalar(ang[:, 2, tb, :], inv_freq[:, :], posf[:, tb:tb + 1], None, ALU.mult)
                settle()
                a2 = ang[:, 2, :, :].rearrange("p a b -> p (a b)")
                c1 = 6.28125
                c2 = float(np.float32(TWO_PI - c1).view(np.uint32).__and__(np.uint32(0xFFFFF000)).view(np.float32))
                c3 = TWO_PI - c1 - c2
                magic = 1.5 * 2.0 ** 23
                for i, shift in enumerate((np.pi / 2, 0.0)):
                    a = ang[:, i, :, :].rearrange("p a b -> p (a b)")
                    turns = cs[:, i, :, :].rearrange("p a b -> p (a b)")
                    V.tensor_scalar(turns, a2, 1 / TWO_PI, shift / TWO_PI, ALU.mult, ALU.add)
                    settle()
                    V.tensor_scalar(turns, turns, magic, None, ALU.add)
                    settle()
                    V.tensor_scalar(turns, turns, magic, None, ALU.subtract)
                    settle()
                    STT(out=a, in0=turns, scalar=-c1, in1=a2, op0=ALU.mult, op1=ALU.add)
                    settle()
                    STT(out=a, in0=turns, scalar=-c2, in1=a, op0=ALU.mult, op1=ALU.add)
                    settle()
                    STT(out=a, in0=turns, scalar=-c3, in1=a, op0=ALU.mult, op1=ALU.add)
                    settle()
                    V.tensor_scalar(a, a, shift, None, ALU.add)
                    settle()
                    V.tensor_scalar(a, a, 3.1415925, -3.1415925, ALU.min, ALU.max)
                settle().then_inc(a_ang, 1)

            def rotations():
                dve.wait_ge(a_cs, 1)
                H2 = HD // 2
                for w in range(2):
                    for i, (f, half) in enumerate(((0, 0), (0, 1), (1, 1), (1, 0))):
                        TT(rot[:, w, i, :, :], cs[:, f, :, :],
                           qkn[:, w, half * H2:(half + 1) * H2].unsqueeze(1).to_broadcast([P, TB, H2]), ALU.mult)
                settle()
            stream("hgrn_out", 0, at.later(32).with_(x_norm("hgrn_out", 2)).put(15, angles).put(18, rotations))

            def sums(g):
                dve.wait_ge(a_sq, g + 2)
                nh = KVH if g < 0 else 8
                V.tensor_reduce(ast[:, 0, 0:TB * nh].rearrange("p (a b) -> p a b", a=TB),
                                asq[:, :, 0:nh * HD].rearrange("p a (b c) -> p a b c", c=HD), AX.X, ALU.add).then_inc(a_ss, 1)

            def rope(g):
                dve.wait_ge(a_std, g + 2)
                nh = KVH if g < 0 else 8
                H2 = HD // 2
                src = (kvtok if g < 0 else aq)[:, :, 0:nh * HD].rearrange("p a (b c) -> p a b c", c=HD)
                V.reciprocal(ast[:, 8, 0:TB * nh], ast[:, 1, 0:TB * nh])
                settle()
                TT(src, src, ast[:, 8, 0:TB * nh].rearrange("p (a b) -> p a b", a=TB).unsqueeze(3).to_broadcast([P, TB, nh, HD]), ALU.mult)
                if g > 0:
                    dve.wait_ge(a_T, g + 1)
                settle()
                r = [rot[:, 1 if g < 0 else 0, i, :, :].unsqueeze(2).to_broadcast([P, TB, nh, H2]) for i in range(4)]
                dst = kdup[:, :, :, 0, :] if g < 0 else ar[:, :, :].rearrange("p a (b c) -> p a b c", c=HD)
                tmp = asq[:, :, 0:nh * HD].rearrange("p a (b c) -> p a b c", c=HD)
                d1, d2, t1, t2 = dst[:, :, :, 0:H2], dst[:, :, :, H2:HD], tmp[:, :, :, 0:H2], tmp[:, :, :, H2:HD]
                x1, x2 = src[:, :, :, 0:H2], src[:, :, :, H2:HD]
                TT(d1, x1, r[0], ALU.mult)
                TT(d2, x2, r[1], ALU.mult)
                TT(t1, x2, r[2], ALU.mult)
                TT(t2, x1, r[3], ALU.mult)
                settle()
                TT(d1, d1, t1, ALU.subtract)
                TT(d2, d2, t2, ALU.add)
                if g < 0:
                    settle()
                    for tb in range(TB):
                        V.tensor_copy(kdup[:, tb, :, 1, :], kdup[:, tb, :, 0, :])
                settle().then_inc(a_rp, 1)

            def masked(g, half):
                for h in range(4 * half, 4 * half + 4):
                    dve.wait_ge(a_s, 8 * g + h + 1)
                    if g and h == 0:
                        dve.wait_ge(a_pt, 8 * g)
                    STT(out=sm[:, h, :], in0=T[:, h % 4, 0:3 * P], scalar=HD ** -0.5, in1=wmask[:, :],
                        op0=ALU.mult, op1=ALU.add).then_inc(a_sm, 1)

            def maxima(g):
                if g:
                    dve.wait_ge(a_sink, g)
                settle()
                V.tensor_reduce(ast[:, 2, 0:8], sm[:, :, 0:P], AX.X, ALU.max)
                V.tensor_reduce(ast[:, 2, 8:16], sm[:, :, P:3 * P], AX.X, ALU.max)
                settle()
                sk = sinks[:, 8 * g:8 * g + 8].unsqueeze(1).to_broadcast([P, 2, 8])
                m = ast[:, 2, :].rearrange("p (a b) -> p a b", a=2)
                TT(m, m, sk, ALU.max)
                settle()
                TT(ast[:, 3, :].rearrange("p (a b) -> p a b", a=2), sk, m, ALU.subtract)
                V.tensor_scalar(ast[:, 2, :], ast[:, 2, :], -1.0, None, ALU.mult)
                settle().then_inc(a_m, 1)

            def finish(g):
                dve.wait_ge(a_o, 8 * g + 8)
                dve.wait_ge(a_sink, g + 1)
                if g:
                    dve.wait_ge(a_yT, g)
                TT(ast[:, 7, :], ast[:, 4, :], ast[:, 5, :], ALU.add)
                settle()
                V.reciprocal(ast[:, 6, :], ast[:, 7, :])
                settle()
                TT(ay[:, :, :].rearrange("p a (b c) -> p (a b) c", c=HD), T23.rearrange("p a (b c) -> p (a b) c", c=HD),
                   ast[:, 6, :].unsqueeze(2).to_broadcast([P, 16, HD]), ALU.mult).then_inc(a_y, 1)

            def y_low(g):
                for b in range(2):
                    dve.wait_ge(a_hi, 2 * g + b + 1)
                    kk = slice(4 * g + 2 * b, 4 * g + 2 * b + 2)
                    low(flat(hy_lo[:, kk, :]), T[:, 2 + b, :], flat(y_hi[:, kk, :]), a_lo)
            at = Hooks()
            for g in range(-1, 4):
                e = 16 + 8 * g
                at.put(e + 2, lambda g=g: sums(g)).put(e + 5, lambda g=g: rope(g))
                if g > 0:
                    at.put(e + 8, lambda g=g: finish(g - 1)).put(e + 10, lambda g=g: y_low(g - 1))
                if g >= 0:
                    at.put(e + 10, lambda g=g: masked(g, 0)).put(e + 11, lambda g=g: masked(g, 1)).put(e + 11, lambda g=g: maxima(g))
            at.put(53, lambda: finish(3)).put(54, lambda: y_low(3))
            stream("kv_q", 0, x_norm("hgrn_out", 2).later(32).with_(at))
            stream("att_out", 0, at.later(40).with_(x_norm("att_out", 3)))

            def u_out(j):
                dve.wait_ge(f_g, j + 1)
                dve.wait_ge(chunk_used, ph["gate_up"].done(j, 1))
                for tb in range(TB):
                    STT(out=fg[:, tb, :], in0=acc[:, ph["gate_up"].pair(1), tb, :], scalar=rs[:, 3, tb:tb + 1], in1=fg[:, tb, :],
                        op0=ALU.mult, op1=ALU.mult).then_inc(pair_free[ph["gate_up"].pair(1)], 1)
                settle().then_inc(f_y, 1)

            def f_lo_out(j):
                for b in range(2):
                    dve.wait_ge(f_h, 2 * j + b + 1)
                    kk = bass.ds(4 * j + 2 * b, 2)
                    low(f_lo[:, kk, :], T[:, b, :].rearrange("p (a b) -> p a b", a=2), f_hi[:, kk, :], f_l)

            def gu(j):
                stream("gate_up", j, x_norm("att_out", 3).later(32) if is_first(j) else
                       Hooks().put(2, lambda: u_out(j - 1)).put(6, lambda: f_lo_out(j - 1)))
            gu(0)
            gu(1)
            with dve.Fori(2, FJ) as j:
                gu(j)
            at = Hooks().put(2, lambda: u_out(FJ - 1)).put(6, lambda: f_lo_out(FJ - 1))
            for k in range(3):
                at.put(ph["down"].end(k) + 2, lambda k=k: residual("down", k))
            stream("down", 0, at)
            residual("down", 3)


def constants():
    i = np.arange(P)
    levels = np.stack([((i[:, None] // (2 * c)) == (i[None] // (2 * c))) & ((i[:, None] // c) != (i[None] // c))
                       for c in LEVELS], 1).astype(np.int32)
    q, k = i[:, None], i[None]
    allowed = np.concatenate([k <= q, k > q, k <= q], 1)
    wmask = np.where(allowed, 0.0, -1e30).astype(np.float32)
    inv = (np.float32(10000.0) ** (-np.arange(0, HD, 2, dtype=np.float32) / np.float32(HD))).astype(np.float32)
    return {"c_ident": np.eye(P, dtype=np.float32), "c_lmask": levels, "c_wmask": wmask, "c_inv_freq": inv[None]}


_INS = ["x", "conv_norm", "conv_w_in", "conv_dw", "conv_dw_b", "conv_ln_g", "conv_ln_b", "conv_w_out", "hgrn_norm",
        "hgrn_w_in", "hgrn_lb_fwd", "hgrn_lb_bwd", "hgrn_o_norm", "hgrn_w_out", "positions_2", "mixer_norm_2",
        "ffn_norm_2", "attn_w_qkv_2", "attn_q_norm_2", "attn_k_norm_2", "attn_sinks_2", "attn_w_o_2", "ffn_w_gate_2",
        "ffn_w_up_2", "ffn_w_down_2"]


def kernel(**inputs):
    import concourse.bacc as _bacc
    from concourse.bass_utils import run_bass_kernel_spmd as _run

    nc = _bacc.Bacc("TRN2", target_bir_lowering=False, num_devices=1)
    arrays, handles = {}, {}
    given = {name: np.ascontiguousarray(inputs[name]) for name in _INS} | constants()
    for name, a in given.items():
        arrays[f"in_{name}_dram"] = a
        handles[name] = nc.dram_tensor(f"in_{name}_dram", a.shape, mybir.dt.from_np(a.dtype), kind="ExternalInput").ap()
    out = nc.dram_tensor("out_0_dram", (1, S, D), F32, kind="ExternalOutput").ap()
    build(nc, handles, out)
    r = _run(nc, [arrays], core_ids=[0])
    return r.results[0]["out_0_dram"]
```
